# Optimizing a Trainium2 kernel written in Bass

```python
import jax, jax.numpy as jnp
from jax import lax
import numpy as np
import math

D_MODEL = 1024
BATCH = 1
SEQ = 256
DEPTH = 2

N_A = DEPTH // 2
N_B = DEPTH - N_A
CHUNK = 64
LEFT_CHUNKS = 8
BAND = (LEFT_CHUNKS + 1) * CHUNK
PAD = LEFT_CHUNKS * CHUNK
D_RNN = D_MODEL
LRU_BLOCKS = 8
LRU_BW = D_RNN // LRU_BLOCKS
CONV_W = 4
LRU_C = 8.0
N_HEADS = 16
HEAD_DIM = D_MODEL // N_HEADS
MAX_REL = 2 * CHUNK
MIN_REL = -(CHUNK - 1)
NREL = MAX_REL - MIN_REL + 1
D_FF = 4 * D_MODEL
EPS = 1e-6


def rmsnorm(x, g):
    xf = x.astype(jnp.float32)
    y = xf * lax.rsqrt(jnp.mean(xf * xf, axis=-1, keepdims=True) + EPS)
    return (y * g.astype(jnp.float32)).astype(x.dtype)

def causal_depthwise_conv(x, w, b):
    s = x.shape[1]
    xp = jnp.pad(x, ((0, 0), (CONV_W - 1, 0), (0, 0)))
    out = b + xp[:, 0:s] * w[0]
    for k in range(1, CONV_W):
        out = out + xp[:, k:k + s] * w[k]
    return out

def rg_lru(x, w_gate, b_gate, lam):
    bsz, s, _ = x.shape
    xf = x.astype(jnp.float32)
    xb = xf.reshape(bsz, s, LRU_BLOCKS, LRU_BW)
    g = jnp.einsum('bsnd,nde->bsne', xb, w_gate.astype(jnp.float32)) + b_gate.astype(jnp.float32)
    r = jax.nn.sigmoid(g[..., :LRU_BW]).reshape(bsz, s, D_RNN)
    i = jax.nn.sigmoid(g[..., LRU_BW:]).reshape(bsz, s, D_RNN)
    log_a = -LRU_C * r * jax.nn.softplus(-lam.astype(jnp.float32))
    a = jnp.exp(log_a)
    b = jnp.sqrt(-jnp.expm1(2.0 * log_a)) * (i * xf)

    def combine(left, right):
        a1, b1 = left
        a2, b2 = right
        return a1 * a2, a2 * b1 + b2

    _, h = lax.associative_scan(combine, (a, b), axis=1)
    return h.astype(x.dtype)

def recurrent_block(x, w_in, conv_w, conv_b, w_gate, b_gate, lam, w_out):
    u = x @ w_in
    gate, rec = u[..., :D_RNN], u[..., D_RNN:]
    rec = causal_depthwise_conv(rec, conv_w, conv_b)
    h = rg_lru(rec, w_gate, b_gate, lam)
    return (jax.nn.gelu(gate) * h) @ w_out

def shared_kv(x, kv_norm, w_kv, k_norm):
    bsz, s, _ = x.shape
    h = rmsnorm(x, kv_norm)
    kv = (h @ w_kv).reshape(bsz, s, 2, N_HEADS, HEAD_DIM)
    k = rmsnorm(kv[:, :, 0], k_norm)
    v = kv[:, :, 1]
    k = jnp.pad(k.transpose(0, 2, 1, 3), ((0, 0), (0, 0), (PAD, 0), (0, 0)))
    v = jnp.pad(v.transpose(0, 2, 1, 3), ((0, 0), (0, 0), (PAD, 0), (0, 0)))
    return k, v

def chunk_band_attention(q, k_pad, v_pad, rel_bias):
    bsz, s = q.shape[:2]
    nc = s // CHUNK
    qc = q.reshape(bsz, nc, CHUNK, N_HEADS, HEAD_DIM).transpose(1, 0, 3, 2, 4)
    qi = jnp.arange(CHUNK)[:, None]
    kj = jnp.arange(BAND)[None, :]
    dist = qi + PAD - kj
    idx = jnp.clip(dist, MIN_REL, MAX_REL) - MIN_REL
    bias = rel_bias.astype(jnp.float32)[:, idx]
    scale = HEAD_DIM ** -0.5

    def one_chunk(args):
        c, qb = args
        kb = lax.dynamic_slice_in_dim(k_pad, c * CHUNK, BAND, axis=2)
        vb = lax.dynamic_slice_in_dim(v_pad, c * CHUNK, BAND, axis=2)
        sc = jnp.einsum('bhqd,bhkd->bhqk', qb, kb).astype(jnp.float32) * scale + bias
        valid = (c * CHUNK - PAD + jnp.arange(BAND)) >= 0
        sc = jnp.where(valid, sc, -jnp.inf)
        p = jax.nn.softmax(sc, axis=-1).astype(vb.dtype)
        return jnp.einsum('bhqk,bhkd->bhqd', p, vb)

    o = lax.map(one_chunk, (jnp.arange(nc), qc))
    return o.transpose(1, 0, 3, 2, 4).reshape(bsz, s, N_HEADS * HEAD_DIM)

def sqrelu_mlp(x, w_up, w_down):
    return jnp.square(jax.nn.relu(x @ w_up)) @ w_down

def first_inputs(seed: int = 0) -> dict:
    key = jax.random.key(seed)
    ks = jax.random.split(key, 24)
    f32 = jnp.float32

    def nrm(k, shape, fan_in):
        return jax.random.normal(k, shape, f32) * (fan_in ** -0.5)

    def gain(k, shape):
        return 1.0 + 0.05 * jax.random.normal(k, shape, f32)

    x = jax.random.normal(ks[0], (BATCH, SEQ, D_MODEL), f32)
    a_norm = gain(ks[1], (N_A, D_MODEL))
    a_w_in = nrm(ks[2], (N_A, D_MODEL, 2 * D_RNN), D_MODEL)
    a_conv_w = nrm(ks[3], (N_A, CONV_W, D_RNN), CONV_W)
    a_conv_b = 0.01 * jax.random.normal(ks[4], (N_A, D_RNN), f32)
    a_w_gate = nrm(ks[5], (N_A, LRU_BLOCKS, LRU_BW, 2 * LRU_BW), LRU_BW)
    a_b_gate = 0.01 * jax.random.normal(ks[6], (N_A, LRU_BLOCKS, 2 * LRU_BW), f32)
    u = jax.random.uniform(ks[7], (N_A, D_RNN), f32, 0.9, 0.999)
    base = u ** (1.0 / LRU_C)
    a_lambda = jnp.log(base) - jnp.log1p(-base)
    a_w_out = nrm(ks[8], (N_A, D_RNN, D_MODEL), D_RNN)
    kv_norm = gain(ks[9], (D_MODEL,))
    w_kv = nrm(ks[10], (D_MODEL, 2 * N_HEADS * HEAD_DIM), D_MODEL)
    k_norm = gain(ks[11], (HEAD_DIM,))
    b_norm = gain(ks[12], (N_B, D_MODEL))
    b_w_q = nrm(ks[13], (N_B, D_MODEL, N_HEADS * HEAD_DIM), D_MODEL)
    b_q_norm = gain(ks[14], (N_B, HEAD_DIM))
    b_rel_bias = 0.1 * jax.random.normal(ks[15], (N_B, N_HEADS, NREL), f32)
    b_w_o = nrm(ks[16], (N_B, N_HEADS * HEAD_DIM, D_MODEL), N_HEADS * HEAD_DIM)
    mlp_norm = gain(ks[17], (DEPTH, D_MODEL))
    w_up = nrm(ks[18], (DEPTH, D_MODEL, D_FF), D_MODEL)
    w_down = nrm(ks[19], (DEPTH, D_FF, D_MODEL), D_FF)
    return {'x': x, 'a_norm': a_norm, 'a_w_in': a_w_in, 'a_conv_w': a_conv_w,
            'a_conv_b': a_conv_b, 'a_w_gate': a_w_gate, 'a_b_gate': a_b_gate,
            'a_lambda': a_lambda, 'a_w_out': a_w_out, 'kv_norm': kv_norm, 'w_kv': w_kv,
            'k_norm': k_norm, 'b_norm': b_norm, 'b_w_q': b_w_q, 'b_q_norm': b_q_norm,
            'b_rel_bias': b_rel_bias, 'b_w_o': b_w_o, 'mlp_norm': mlp_norm,
            'w_up': w_up, 'w_down': w_down}

def first_block(x, a_norm, a_w_in, a_conv_w, a_conv_b, a_w_gate, a_b_gate, a_lambda,
              a_w_out, kv_norm, w_kv, k_norm, b_norm, b_w_q, b_q_norm, b_rel_bias,
              b_w_o, mlp_norm, w_up, w_down):
    bsz, s, _ = x.shape
    h = x
    k_pad = None
    v_pad = None
    for l in range(DEPTH):
        if l < N_A:
            h = h + recurrent_block(rmsnorm(h, a_norm[l]), a_w_in[l], a_conv_w[l], a_conv_b[l],
                                    a_w_gate[l], a_b_gate[l], a_lambda[l], a_w_out[l])
        else:
            if l == N_A:
                k_pad, v_pad = shared_kv(h, kv_norm, w_kv, k_norm)
            j = l - N_A
            q = (rmsnorm(h, b_norm[j]) @ b_w_q[j]).reshape(bsz, s, N_HEADS, HEAD_DIM)
            q = rmsnorm(q, b_q_norm[j])
            o = chunk_band_attention(q, k_pad, v_pad, b_rel_bias[j])
            h = h + o @ b_w_o[j]
        h = h + sqrelu_mlp(rmsnorm(h, mlp_norm[l]), w_up[l], w_down[l])
    return h


DEPTH_2 = 1

MOBA_HEADS = 8
MOBA_HEAD_DIM = 64
MOBA_BLOCK = 256
MOBA_TOPK = 3
MOBA_QCHUNK = 64
SWA_Q_HEADS = 8
SWA_KV_HEADS = 2
SWA_HEAD_DIM = 64
SWA_WINDOW = 128
SWA_BLOCK = 128
MEM_HEADS = 4
MEM_HEAD_DIM = 128
MEM_LEN = 256
NUM_BUCKETS = 32
MAX_EXACT = NUM_BUCKETS // 2
REL_MAX_DISTANCE = 128
N_SELF_HEADS = MOBA_HEADS + SWA_Q_HEADS
FFN_HIDDEN = 2816
CONV_WIDTH = 3
RMS_EPS = 1e-6
MOBA_W = MOBA_HEADS * MOBA_HEAD_DIM
SWA_QW = SWA_Q_HEADS * SWA_HEAD_DIM
SWA_KVW = SWA_KV_HEADS * SWA_HEAD_DIM
MEM_W = MEM_HEADS * MEM_HEAD_DIM
IN_SPLITS = (MOBA_W, MOBA_W, MOBA_W, SWA_QW, SWA_KVW, SWA_KVW, MEM_W, D_MODEL, D_MODEL, D_MODEL)
IN_WIDTH = 3 * MOBA_W + SWA_QW + 2 * SWA_KVW + MEM_W + 3 * D_MODEL


def rmsnorm_2(x, g):
    xf = x.astype(jnp.float32)
    r = lax.rsqrt(jnp.mean(xf * xf, axis=-1, keepdims=True) + RMS_EPS)
    return (xf * r * g.astype(jnp.float32)).astype(x.dtype)

def t5_bucket(dist):
    n = jnp.maximum(dist, 0)
    nf = jnp.maximum(n, 1).astype(jnp.float32)
    large = MAX_EXACT + (jnp.log(nf / MAX_EXACT) / math.log(REL_MAX_DISTANCE / MAX_EXACT)
                         * (NUM_BUCKETS - MAX_EXACT)).astype(jnp.int32)
    large = jnp.minimum(large, NUM_BUCKETS - 1)
    return jnp.where(n < MAX_EXACT, n, large)

def moba_attention(q, k, v, bias_table):
    B_, S_, H, dh = q.shape
    Sp = -(-S_ // MOBA_BLOCK) * MOBA_BLOCK
    pad = Sp - S_
    if pad:
        padw = ((0, 0), (0, pad), (0, 0), (0, 0))
        q, k, v = jnp.pad(q, padw), jnp.pad(k, padw), jnp.pad(v, padw)
    NB = Sp // MOBA_BLOCK
    scale = 1.0 / math.sqrt(dh)
    qh = q.transpose(0, 2, 1, 3)
    kb = k.reshape(B_, NB, MOBA_BLOCK, H, dh).transpose(0, 3, 1, 2, 4)
    vb = v.reshape(B_, NB, MOBA_BLOCK, H, dh).transpose(0, 3, 1, 2, 4)
    kmean = jnp.mean(kb.astype(jnp.float32), axis=3)
    gate = jnp.einsum('bhsd,bhnd->bhsn', qh.astype(jnp.float32), kmean)
    qblk = jnp.arange(Sp) // MOBA_BLOCK
    past = jnp.arange(NB)[None, :] < qblk[:, None]
    gate = jnp.where(past, gate, -jnp.inf)
    k_sel = min(MOBA_TOPK, NB)
    _, sel = lax.top_k(gate, k_sel)
    sel_valid = jnp.arange(k_sel)[None, :] < qblk[:, None]
    bi = jnp.arange(B_)[:, None, None, None]
    hi = jnp.arange(H)[None, :, None, None]
    hb = jnp.arange(H)[None, :, None, None, None]
    kpos_in = jnp.arange(MOBA_BLOCK)

    def chunk(i):
        q0 = i * MOBA_QCHUNK
        qc = lax.dynamic_slice_in_dim(qh, q0, MOBA_QCHUNK, axis=2)
        selc = lax.dynamic_slice_in_dim(sel, q0, MOBA_QCHUNK, axis=2)
        validc = lax.dynamic_slice_in_dim(sel_valid, q0, MOBA_QCHUNK, axis=0)
        c = q0 // MOBA_BLOCK
        kg = kb[bi, hi, selc]
        vg = vb[bi, hi, selc]
        k_own = lax.dynamic_index_in_dim(kb, c, axis=2, keepdims=False)
        v_own = lax.dynamic_index_in_dim(vb, c, axis=2, keepdims=False)
        qpos = q0 + jnp.arange(MOBA_QCHUNK)
        kpos_sel = selc[..., None] * MOBA_BLOCK + kpos_in
        s_sel = (jnp.einsum('bhqd,bhqnkd->bhqnk', qc, kg).astype(jnp.float32) * scale
                 + bias_table[hb, t5_bucket(qpos[:, None, None] - kpos_sel)].astype(jnp.float32))
        s_sel = jnp.where(validc[:, :, None], s_sel, -jnp.inf)
        dist_own = qpos[:, None] - (c * MOBA_BLOCK + kpos_in)[None, :]
        s_own = (jnp.einsum('bhqd,bhkd->bhqk', qc, k_own).astype(jnp.float32) * scale
                 + bias_table[:, t5_bucket(dist_own)].astype(jnp.float32))
        s_own = jnp.where(dist_own >= 0, s_own, -jnp.inf)
        s_all = jnp.concatenate(
            [s_sel.reshape(B_, H, MOBA_QCHUNK, k_sel * MOBA_BLOCK), s_own], axis=-1)
        p = jax.nn.softmax(s_all, axis=-1).astype(v.dtype)
        p_sel = p[..., :k_sel * MOBA_BLOCK].reshape(B_, H, MOBA_QCHUNK, k_sel, MOBA_BLOCK)
        p_own = p[..., k_sel * MOBA_BLOCK:]
        return (jnp.einsum('bhqnk,bhqnkd->bhqd', p_sel, vg)
                + jnp.einsum('bhqk,bhkd->bhqd', p_own, v_own))

    outs = lax.map(chunk, jnp.arange(Sp // MOBA_QCHUNK))
    out = outs.transpose(1, 0, 3, 2, 4).reshape(B_, Sp, H, dh)
    return out[:, :S_]

def swa_attention(q, k, v, sinks, bias_table):
    B_, S_, HQ, dh = q.shape
    HKV = k.shape[2]
    G = HQ // HKV
    QB = SWA_BLOCK
    nblk = S_ // QB
    scale = 1.0 / math.sqrt(dh)
    qb = q.reshape(B_, nblk, QB, HKV, G, dh)
    kb = k.reshape(B_, nblk, QB, HKV, dh)
    vb = v.reshape(B_, nblk, QB, HKV, dh)
    padw = ((0, 0), (1, 0), (0, 0), (0, 0), (0, 0))
    kband = jnp.concatenate([jnp.pad(kb, padw)[:, :-1], kb], axis=2)
    vband = jnp.concatenate([jnp.pad(vb, padw)[:, :-1], vb], axis=2)
    s = jnp.einsum('bnqhgd,bnkhd->bhgnqk', qb, kband).astype(jnp.float32) * scale
    dist = QB + jnp.arange(QB)[:, None] - jnp.arange(2 * QB)[None, :]
    bias = bias_table[:, t5_bucket(dist)].astype(jnp.float32).reshape(HKV, G, 1, QB, 2 * QB)
    s = s + bias
    kpos = (jnp.arange(nblk)[:, None] - 1) * QB + jnp.arange(2 * QB)[None, :]
    allowed = ((dist >= 0) & (dist < SWA_WINDOW))[None] & (kpos >= 0)[:, None, :]
    s = jnp.where(allowed, s, -jnp.inf)
    sink = sinks.astype(jnp.float32).reshape(HKV, G, 1, 1, 1)
    m = jnp.maximum(jnp.max(s, axis=-1, keepdims=True), sink)
    p = jnp.exp(s - m)
    denom = jnp.sum(p, axis=-1, keepdims=True) + jnp.exp(sink - m)
    p = (p / denom).astype(v.dtype)
    o = jnp.einsum('bhgnqk,bnkhd->bnqhgd', p, vband)
    return o.reshape(B_, S_, HQ * dh)

def memory_attention(q, km, vm):
    B_, S_, Hm, dm = q.shape
    s = jnp.einsum('bshd,bmhd->bhsm', q, km).astype(jnp.float32) * (1.0 / math.sqrt(dm))
    p = jax.nn.softmax(s, axis=-1).astype(vm.dtype)
    return jnp.einsum('bhsm,bmhd->bshd', p, vm).reshape(B_, S_, Hm * dm)

def causal_depthwise_conv_2(u, w, b):
    S_ = u.shape[1]
    up = jnp.pad(u, ((0, 0), (CONV_WIDTH - 1, 0), (0, 0)))
    out = b.astype(u.dtype)
    for t in range(CONV_WIDTH):
        out = out + w[t].astype(u.dtype) * up[:, t:t + S_]
    return out

def _normal(k, shape, scale):
    return jax.random.normal(k, shape, jnp.float32) * scale

def second_inputs(seed: int = 0) -> dict:
    key = jax.random.key(seed)
    ks = jax.random.split(key, 20)
    L, D, F = DEPTH_2, D_MODEL, FFN_HIDDEN
    return {
        "x": _normal(ks[0], (BATCH, SEQ, D), 1.0),
        "mem": _normal(ks[1], (BATCH, MEM_LEN, D), 1.0),
        "norm_mix_pre": 1.0 + _normal(ks[2], (L, D), 0.05),
        "norm_mix_post": 1.0 + _normal(ks[3], (L, D), 0.05),
        "norm_ffn_pre": 1.0 + _normal(ks[4], (L, D), 0.05),
        "norm_ffn_post": 1.0 + _normal(ks[5], (L, D), 0.05),
        "norm_mem": 1.0 + _normal(ks[6], (L, D), 0.05),
        "w_in": _normal(ks[7], (L, D, IN_WIDTH), D ** -0.5),
        "rel_bias": _normal(ks[8], (NUM_BUCKETS, N_SELF_HEADS), 0.3),
        "swa_sinks": _normal(ks[9], (L, SWA_Q_HEADS), 1.0),
        "w_mem_kv": _normal(ks[10], (L, D, 2 * MEM_W), D ** -0.5),
        "w_branch_moba": _normal(ks[11], (L, MOBA_W, D), MOBA_W ** -0.5),
        "w_branch_swa": _normal(ks[12], (L, SWA_QW, D), SWA_QW ** -0.5),
        "w_branch_mem": _normal(ks[13], (L, MEM_W, D), MEM_W ** -0.5),
        "w_out": _normal(ks[14], (L, D, D), D ** -0.5),
        "w_ffn_up": _normal(ks[15], (L, D, 2 * F), D ** -0.5),
        "ffn_conv_w": _normal(ks[16], (L, CONV_WIDTH, 2 * F), CONV_WIDTH ** -0.5),
        "ffn_conv_b": _normal(ks[17], (L, 2 * F), 0.02),
        "w_ffn_down": _normal(ks[18], (L, F, D), F ** -0.5),
    }

def second_block(x, mem, norm_mix_pre, norm_mix_post, norm_ffn_pre, norm_ffn_post, norm_mem,
              w_in, rel_bias, swa_sinks, w_mem_kv, w_branch_moba, w_branch_swa, w_branch_mem,
              w_out, w_ffn_up, ffn_conv_w, ffn_conv_b, w_ffn_down):
    B_, S_, _ = x.shape
    cuts = []
    acc = 0
    for width in IN_SPLITS[:-1]:
        acc += width
        cuts.append(acc)
    bias_moba = rel_bias[:, :MOBA_HEADS].T
    bias_swa = rel_bias[:, MOBA_HEADS:].T
    for l in range(DEPTH_2):
        h = rmsnorm_2(x, norm_mix_pre[l])
        proj = h @ w_in[l]
        (q_mb, k_mb, v_mb, q_sw, k_sw, v_sw, q_me,
         g_mb, g_sw, g_me) = jnp.split(proj, cuts, axis=-1)
        o_mb = moba_attention(
            q_mb.reshape(B_, S_, MOBA_HEADS, MOBA_HEAD_DIM),
            k_mb.reshape(B_, S_, MOBA_HEADS, MOBA_HEAD_DIM),
            v_mb.reshape(B_, S_, MOBA_HEADS, MOBA_HEAD_DIM), bias_moba).reshape(B_, S_, MOBA_W)
        o_sw = swa_attention(
            q_sw.reshape(B_, S_, SWA_Q_HEADS, SWA_HEAD_DIM),
            k_sw.reshape(B_, S_, SWA_KV_HEADS, SWA_HEAD_DIM),
            v_sw.reshape(B_, S_, SWA_KV_HEADS, SWA_HEAD_DIM), swa_sinks[l], bias_swa)
        kv_me = rmsnorm_2(mem, norm_mem[l]) @ w_mem_kv[l]
        M_ = mem.shape[1]
        k_me = kv_me[..., :MEM_W].reshape(B_, M_, MEM_HEADS, MEM_HEAD_DIM)
        v_me = kv_me[..., MEM_W:].reshape(B_, M_, MEM_HEADS, MEM_HEAD_DIM)
        o_me = memory_attention(q_me.reshape(B_, S_, MEM_HEADS, MEM_HEAD_DIM), k_me, v_me)
        merged = (jax.nn.sigmoid(g_mb) * (o_mb @ w_branch_moba[l])
                  + jax.nn.sigmoid(g_sw) * (o_sw @ w_branch_swa[l])
                  + jax.nn.sigmoid(g_me) * (o_me @ w_branch_mem[l]))
        x = x + rmsnorm_2(merged @ w_out[l], norm_mix_post[l])
        h = rmsnorm_2(x, norm_ffn_pre[l])
        u = causal_depthwise_conv_2(h @ w_ffn_up[l], ffn_conv_w[l], ffn_conv_b[l])
        u_gate, u_val = jnp.split(u, 2, axis=-1)
        y = (jax.nn.gelu(u_gate, approximate=True) * u_val) @ w_ffn_down[l]
        x = x + rmsnorm_2(y, norm_ffn_post[l])
    return x


def setup_inputs(seed=0):
    out = dict(first_inputs(seed))
    for name, value in second_inputs(seed + 1).items():
        if name != "x":
            out[name + "_2"] = value
    return out


def reference(
    x, a_norm, a_w_in, a_conv_w, a_conv_b, a_w_gate, a_b_gate, a_lambda, a_w_out, kv_norm, w_kv,
    k_norm, b_norm, b_w_q, b_q_norm, b_rel_bias, b_w_o, mlp_norm, w_up, w_down, mem_2,
    norm_mix_pre_2, norm_mix_post_2, norm_ffn_pre_2, norm_ffn_post_2, norm_mem_2, w_in_2,
    rel_bias_2, swa_sinks_2, w_mem_kv_2, w_branch_moba_2, w_branch_swa_2, w_branch_mem_2,
    w_out_2, w_ffn_up_2, ffn_conv_w_2, ffn_conv_b_2, w_ffn_down_2,
):
    x = first_block(
        x, a_norm, a_w_in, a_conv_w, a_conv_b, a_w_gate, a_b_gate, a_lambda, a_w_out, kv_norm,
        w_kv, k_norm, b_norm, b_w_q, b_q_norm, b_rel_bias, b_w_o, mlp_norm, w_up, w_down,
    )
    return second_block(
        x, mem_2, norm_mix_pre_2, norm_mix_post_2, norm_ffn_pre_2, norm_ffn_post_2, norm_mem_2,
        w_in_2, rel_bias_2, swa_sinks_2, w_mem_kv_2, w_branch_moba_2, w_branch_swa_2,
        w_branch_mem_2, w_out_2, w_ffn_up_2, ffn_conv_w_2, ffn_conv_b_2, w_ffn_down_2,
    )


_drawn_inputs = setup_inputs


def setup_inputs(seed=0):
    import zlib

    import numpy as np

    out = dict(_drawn_inputs(seed))
    spreads = {}
    factors = {'a_b_gate': 8.0,
     'kv_norm': 3.765,
     'k_norm': 8.0,
     'b_norm': 8.0,
     'b_q_norm': 8.0,
     'b_rel_bias': 6.947,
     'norm_ffn_post_2': 7.733,
     'norm_mem_2': 8.0,
     'swa_sinks_2': 33.808,
     'ffn_conv_b_2': 4.705,
     'norm_mix_post_2': 4.293,
     'rel_bias_2': 8.0,
     'w_branch_moba_2': 3.237,
     'w_branch_swa_2': 3.695}
    for name, (base, spread) in spreads.items():
        noise = np.random.default_rng([zlib.crc32(name.encode()), seed]).standard_normal(out[name].shape)
        drawn = base * np.exp(spread * noise) if base else spread * noise
        out[name] = __import__('jax').numpy.asarray(drawn.astype(out[name].dtype))
    for name, factor in factors.items():
        out[name] = (out[name] * factor).astype(out[name].dtype)
    return out
```

```python
from contextlib import ExitStack

import numpy as np

import concourse.bass as bass
from concourse import mybir

F32 = mybir.dt.float32
F32R = mybir.dt.float32r
ALU = mybir.AluOpType
ACT = mybir.ActivationFunctionType
AX_X = mybir.AxisListType.X

P = 128
T = 256
TT = T // P
D = 1024
KT = D // P
EPS = 1e-6
D_FF = 4096
FFN = 2816
CHUNK = 64
NREL = 192
MASKED = -1.0e30
LRU_C = 8.0
SLOTS = 4
LEAD = 3
UNIT = 2048

U_REC, U_LRU = 0, 5
U_GATE = [4, 6, 7, 8]
U_MEMK, U_MEMV, U_ROUT = 9, 11, 13
U_MLP0 = 17
U_K, U_Q, U_V, U_O = 49, 53, 57, 61
U_MLP1 = 65
U_QKV = 97
U_G2 = [108, 112, 118]
U_BR = [116, 122, 124]
U_SWQ = (103, 104)
U_OUT2 = 126
U_FFN = 130
N_UNITS = 163
MLP_UNITS = 32
FFN_STEPS = FFN // 256

G_REC, G_GATE, G_MEMK = 0, 8, 16
G_MLP0, G_MLP1 = 20, 52
G_QMB, G_KMB, G_QSW, G_KSW, G_QME = 84, 88, 92, 96, 97
G_G2 = [101, 109, 125]
G_BR = [117, 133, 141]
G_FFN = 149


def steps_of_units():
    n = []
    for u in range(N_UNITS):
        if u == U_LRU:
            n.append(8)
        elif u < U_MEMV:
            n.append(2)
        elif U_MLP0 <= u < U_K or U_MLP1 <= u < U_QKV:
            v = u - (U_MLP0 if u < U_K else U_MLP1)
            n.append(2 if v == 0 or (v % 2 and v < MLP_UNITS - 1) else 1)
        elif U_QKV <= u < U_G2[0]:
            n.append([2, 2, 2, 2, 1, 1, 2, 2, 2, 2, 2][u - U_QKV])
        elif U_G2[0] <= u < U_OUT2:
            n.append(4 if any(v <= u < v + 2 for v in U_BR) else 2)
        elif u >= U_FFN:
            v = u - U_FFN
            n.append(2 if v < 2 or (v < N_UNITS - U_FFN - 1 and (v - 2) % 3 < 2) else 1)
        else:
            n.append(1)
    return n


STEPS = steps_of_units()
AFTER = [sum(STEPS[:u + 1]) for u in range(N_UNITS)]


def LANDED(u):
    return 16 * (u // SLOTS + 1) + 16 * sum(v <= u and v % SLOTS == u % SLOTS for v in U_SWQ)


def BEFORE(u):
    return AFTER[u - 1] if u else 0


B_MEMV, B_K, B_Q, B_V, B_VMB, B_VSW = range(6)
A_ROUT, A_MLP0, A_O, A_MLP1, A_OUT2, A_FFN = range(6)
SQ_NORM = [0, 1, 2, 3, 4, 5, 7]
SQ_POST = [6, 8]
ROOTS = [0, 2, 4, 6, 10, 12, 14, 16, 18]
ROOTS_KQ = [8, 9]
KO = [0, 4, 1, 5, 2, 6, 3, 7]


def bank_of(g):
    if g in [f + i for f in (G_REC, G_MLP0, G_MLP1, G_QMB, G_FFN) for i in range(2)]:
        return 4 + g % 2
    return g % 2 if G_G2[0] <= g < G_FFN else g % 4


def ring_of(g):
    return 2 if G_G2[0] <= g < G_FFN else 4


R_ANORM, R_KV, R_B, R_MLP, R_MIX, R_FFN, R_MEM, R_CB, R_CW, R_LAM, R_BG = 0, 8, 16, 24, 40, 48, 56, 64, 72, 104, 112
NT = FFN * 2 // P


def bass_blocks(nc, A, out):
    w_units = []

    def cols(w, k, c0):
        return w[:, c0:c0 + 256].rearrange("(k p) n -> p k n", p=P)

    def rows(w, r0, n=2, c0=0, nn=D):
        return w[r0:r0 + n * P, c0:c0 + nn].rearrange("(k p) n -> p k n", p=P)

    a_in = A["a_w_in"][0]
    w_in2 = A["w_in_2"][0]
    w_kv = A["w_kv"]
    w_mem = A["w_mem_kv_2"][0]
    w_units += [cols(a_in, KT, D + 256 * i) for i in range(4)]
    w_units += [cols(a_in, KT, 0), A["a_w_gate"][0].rearrange("k p n -> p k n")]
    w_units += [cols(a_in, KT, 256 * i) for i in range(1, 4)]
    w_units += [cols(w_mem, KT, 256 * i) for i in range(2)]
    w_units += [rows(w_mem, 512 * i, 4, 512, 512) for i in range(2)]
    w_units += [rows(A["a_w_out"][0], 256 * i) for i in range(4)]

    def mlp_units(layer):
        up = [cols(A["w_up"][layer], KT, 256 * i) for i in range(16)]
        down = [rows(A["w_down"][layer], 256 * i) for i in range(16)]
        us = [up[0]]
        for i in range(15):
            us += [up[i + 1], down[i]]
        return us + [down[15]]

    w_units += mlp_units(0)
    w_units += [rows(w_kv, 256 * i) for i in range(4)]
    w_units += [rows(A["b_w_q"][0], 256 * i) for i in range(4)]
    w_units += [rows(w_kv, 256 * i, 2, D, D) for i in range(4)]
    w_units += [rows(A["b_w_o"][0], 256 * i) for i in range(4)]
    w_units += mlp_units(1)
    w_units += [cols(w_in2, KT, 256 * i) for i in range(4)]
    w_units += [rows(w_in2, 512 * i, 4, 1024, 512) for i in range(2)]
    w_units += [w_in2[:, 1536:2048].rearrange("(k p) (h n) -> p k h n", p=P, h=2)[:, :, :, P * i:P * i + P]
                for i in range(2)]
    w_units += [cols(w_in2, KT, 2048 + 256 * i) for i in range(3)]
    gates2 = lambda b: [cols(w_in2, KT, 2816 + D * b + 256 * i) for i in range(4)]
    branch = lambda name: [rows(A[name][0], 0, 4, 512 * i, 512) for i in range(2)]
    w_units += gates2(0) + gates2(1) + branch("w_branch_moba_2") + gates2(2)
    w_units += branch("w_branch_swa_2") + branch("w_branch_mem_2")
    w_units += [rows(A["w_out_2"][0], 256 * i) for i in range(4)]
    up2, down2 = A["w_ffn_up_2"][0], A["w_ffn_down_2"][0]
    pair = lambda j: [cols(up2, KT, 256 * j), cols(up2, KT, FFN + 256 * j)]
    w_units += pair(0)
    for j in range(FFN_STEPS - 1):
        w_units += pair(j + 1) + [rows(down2, 256 * j)]
    w_units += [rows(down2, 256 * (FFN_STEPS - 1))]
    assert len(w_units) == N_UNITS

    ctx = ExitStack()
    with ctx:
        def sb(name, shape, dt=F32):
            return ctx.enter_context(nc.sbuf_tensor(name, shape, dt))

        def sem(name):
            return ctx.enter_context(nc.semaphore(name))

        bias_rows = nc.dram_tensor("bias_rows", [32, 384], F32, kind="Internal").ap()

        raw = sb("raw", [P, SLOTS, UNIT])
        whi = sb("whi", [P, SLOTS, UNIT], F32R)
        wlo = sb("wlo", [P, SLOTS, UNIT], F32R)
        res = sb("res", [P, TT, D])
        XA = sb("XA", [P, KT, 2, T], F32R)
        XB = sb("XB", [P, KT, 2, T], F32R)
        kT_me = sb("kT_me", [P, 4, T])
        v_me = sb("v_me", [P, TT, 512])
        arena = sb("arena", [P, 5 * 2048 + 2072 + 2048])
        tmp = sb("tmp", [P, 4, T])
        ident = sb("ident", [P, P])
        vecs = sb("vecs", [P, P])
        fvec = sb("fvec", [P, 2, 88])
        headg = sb("headg", [P, 2])
        sinks = sb("sinks", [P, 8])
        sp_a = sb("sp_a", [P, 8])
        sp_b = sb("sp_b", [P, 8])
        sp_c = sb("sp_c", [P, 8])
        cneg = sb("cneg", [P, 8])
        cpos = sb("cpos", [P, 8])
        ss = sb("ss", [P, 64])
        rstd = sb("rstd", [P, 32])
        mhalf = sb("mhalf", [P, 32])
        smax = sb("smax", [P, 3, 2])
        snmax = sb("snmax", [P, 3, 2])
        ssum = sb("ssum", [P, 3, 2])
        ssink = sb("ssink", [P, 3, 2])
        srec = sb("srec", [P, 3, 2])
        PS = ctx.enter_context(nc.psum_tensor("PS", [P, 8, 512], F32))

        def area(o, n):
            return arena[:, o:o + n]

        S = [2048 * i for i in range(5)]
        XRO = 5 * 2048
        AO = XRO + 2072
        xn = area(S[0], 2048).rearrange("p (t n) -> p t n", t=TT)
        xrec = area(XRO, 8 * 259).rearrange("p (k n) -> p k n", k=8)
        xc = area(S[1], 2048).rearrange("p (k n) -> p k n", k=8)
        gate = area(S[2], 2048).rearrange("p (k n) -> p k n", k=8)
        rg = area(S[3], 2048).rearrange("p (k n) -> p k n", k=8)
        ig = area(S[4], 2048).rearrange("p (k n) -> p k n", k=8)
        av = area(AO, 2048).rearrange("p (k n) -> p k n", k=8)
        sq = area(XRO, 2048).rearrange("p (k n) -> p k n", k=8)
        up = area(S[1], 1024).rearrange("p (b m n) -> p b m n", b=2, m=2)
        kT = area(S[1], 2048).rearrange("p (k n) -> p k n", k=8)
        qT = area(S[2], 2048).rearrange("p (k n) -> p k n", k=8)
        vtok = area(S[3], 2048).rearrange("p (t n) -> p t n", t=TT)
        kq = area(S[4], 2048).rearrange("p (t n) -> p t n", t=TT)
        bias1 = area(XRO, 4096).rearrange("p (h n) -> p h n", h=16)
        prob3 = area(S[0], 1152).rearrange("p (b n) -> p b n", b=3)
        probT3 = area(S[0] + 1152, 768).rearrange("p (b n) -> p b n", b=2)
        prob_me = area(S[0], 1024).rearrange("p (b n) -> p b n", b=2)
        probT_me = area(S[0] + 1024, 1024).rearrange("p (b n) -> p b n", b=2)
        qT_mb = area(S[1], 1024).rearrange("p (k n) -> p k n", k=4)
        kT_mb = area(S[1] + 1024, 1024).rearrange("p (k n) -> p k n", k=4)
        qT_sw = area(S[2], 1024).rearrange("p (k n) -> p k n", k=4)
        qT_me = area(S[2] + 1024, 1024).rearrange("p (k n) -> p k n", k=4)
        v_mb = area(S[3], 1024).rearrange("p (t n) -> p t n", t=TT)
        kT_sw = area(S[3] + 1024, T)
        v_sw = area(S[3] + 1536, 256).rearrange("p (t n) -> p t n", t=TT)
        gA, gB = (area(o, 2048).rearrange("p (k n) -> p k n", k=8) for o in (S[4], XRO))
        g_br = [gA, gB, gA]
        merged = kT
        fu = area(S[1], 4 * 258).rearrange("p (k n) -> p k n", k=4)
        fc = area(S[2], 4 * 256).rearrange("p (k n) -> p k n", k=4)
        gpost = area(S[3], 2048).rearrange("p (t n) -> p t n", t=2)
        rows_in = area(S[1], 512).rearrange("p (k n) -> p k n", k=4)
        erow = area(S[2], 768).rearrange("p (k n) -> p k n", k=2)
        onehot = area(S[3], 384)
        relb = area(S[3] + 512, 16)

        s_landed = [sem(f"landed{i}") for i in range(SLOTS)]
        s_hi = sem("split_hi")
        s_lo = sem("split_lo")
        s_step = sem("pe_steps")
        s_tmp = sem("group_tmp")
        s_evac = sem("group_evac")
        s_bev = sem("token_evac")
        s_tok = sem("piece_done")
        s_add = sem("piece_added")
        s_ss, s_ms, s_rstd = sem("sumsq"), sem("meansq_kq"), sem("rstd_ready")
        s_xn, s_xnT = sem("xn_ready"), sem("xn_transposed")
        s_xhi, s_xlo = sem("x_hi"), sem("x_lo")
        s_chain = sem("dve_chain")
        s_achain = sem("act_chain")
        s_pchain = sem("pool_chain")
        s_const = sem("constants")
        s_ident = sem("identity")
        s_small = sem("small_loads")
        s_x = sem("x_loaded")
        s_mem = sem("mem_loaded")
        s_vT, s_vec = sem("vectors_transposed"), sem("vectors_ready")
        s_e1, s_eps, s_e2 = sem("rel_rows"), sem("rel_psum"), sem("rel_rows2")
        s_ew = sem("bias_rows_written")
        s_b1l, s_b1 = sem("bias1_loaded"), sem("bias1_masked")
        s_b2l, s_b2 = sem("bias2_loaded"), sem("bias2_masked")
        s_sp0, s_sp1, s_spz, s_cc = sem("softplus_in"), sem("softplus_in2"), sem("softplus_exp"), sem("decay_scale")
        s_convd, s_ch, s_cl = sem("conv_done"), sem("conv_hi"), sem("conv_lo")
        s_lru = sem("lru_gates")
        s_ix, s_tap = sem("gated_input"), sem("conv_first_tap")
        s_a, s_q, s_sq, s_scan, s_gelu, s_y, s_yh, s_yl = (
            sem("decay"), sem("input_scale2"), sem("input_scale"), sem("scanned"), sem("gelu_gate"),
            sem("rec_out"), sem("rec_out_hi"), sem("rec_out_lo"))
        s_relu, s_hh, s_hl = sem("hidden"), sem("hidden_hi"), sem("hidden_lo")
        s_kq2, s_kqn, s_kqT, s_kqev = (
            sem("kq_squares"), sem("kq_normed"), sem("kq_transposed"), sem("kq_evac"))
        s_S, s_Sfree, s_max, s_exp, s_p, s_pt, s_ptc, s_pv = (
            sem("scores"), sem("scores_read"), sem("row_max"), sem("exps"), sem("probs"),
            sem("probs_transposed"), sem("probsT"), sem("pv"))
        s_ohi, s_olo = sem("attn_hi"), sem("attn_lo")
        s_sig = sem("gates_sigmoid")
        s_mdone, s_mh, s_ml = sem("merged"), sem("merged_hi"), sem("merged_lo")
        s_conv2, s_gelu2, s_prod, s_fh, s_fl = (
            sem("ffn_conv"), sem("ffn_gelu"), sem("ffn_prod"), sem("ffn_hi"), sem("ffn_lo"))
        s_gp = sem("post_gains")
        s_out = sem("out_written")

        block = ctx.enter_context(nc.Block())

        W8 = lambda w, s: w[:, s, :].rearrange("p (k n) -> p k n", k=KT)
        W2 = lambda w, s: w[:, s, :].rearrange("p (k n) -> p k n", k=2)
        W4 = lambda w, s: w[:, s, :].rearrange("p (k n) -> p k n", k=4)

        def swq(w, s, j):
            v = w[:, s, :]
            return (v.rearrange("p (k j h n) -> p k j h n", k=KT, j=2, h=2)[:, :, j],
                    v.rearrange("p (k h j n) -> p k h j n", k=KT, h=2, j=2)[:, :, :, j])

        def mlp_base(layer):
            return (U_MLP0, G_MLP0, 0) if layer == 0 else (U_MLP1, G_MLP1, 16)

        def out_of(H):
            return H // 2 if H < 32 else 16 + (H - 32)

        def ends_out(H):
            return H >= 32 or H % 2 == 1

        def attn_dst(o):
            return (XB, o) if o < 8 else (XB, (o - 8) % 8)

        N_SMALL = 22
        ubr = area(S[2], 1024).rearrange("p (b n) -> p b n", b=4)

        def xnT(bank, k):
            b = bank + 2 * (k // 4)
            return PS[:, b:b + 2, P * (k % 4):P * (k % 4) + P]

        def place_of(H):
            if H < 32:
                return prob3[:, H % 3, :], probT3[:, H % 2, :], H % 3
            return prob_me[:, H % 2, :], probT_me[:, H % 2, :], H % 3

        def score_bank(H):
            return (2, 3, 0)[H % 3] if H < 16 else 2 + H % 2

        def scored_before(H):
            return H - 2 if H < 16 else H - 1

        def pieces(bank0=4):
            return [(t, c, bank0 + 2 * t + c) for t in range(TT) for c in range(2)]

        NORM_HI = [8 * n + (8 if n > 3 else 0) for n in range(8)]

        @block.sync
        def _(sp):
            sp.dma_start(res[:], A["x"][0].rearrange("(t p) n -> p t n", p=P)).then_inc(s_x, 16)

            def load(u, slot, value):
                if value is not None:
                    sp.wait_ge(s_lo, value)
                dst = raw[:, slot, :].rearrange("p (k n) -> p k n", k=w_units[u].shape[1])
                if u in U_SWQ:
                    for h in range(2):
                        sp.dma_start(dst[:, :, P * h:P * h + P], w_units[u][:, :, h, :]).then_inc(s_landed[slot], 16)
                    return
                sp.dma_start(dst, w_units[u]).then_inc(s_landed[slot], 16)

            for u in range(N_UNITS):
                load(u, u % SLOTS, u - SLOTS + 1 if u >= SLOTS else None)
                if u == 3:
                    sp.wait_ge(s_xnT, 1)
                    sp.dma_start(xn, A["mem_2"][0].rearrange("(t p) n -> p t n", p=P)).then_inc(s_mem, 16)
            for t in range(TT):
                sp.wait_ge(s_add, 4 * A_FFN + 2 * t + 2)
                sp.dma_start(out[0, P * t:P * t + P, :], res[:, t, :]).then_inc(s_out, 16)
            sp.wait_ge(s_out, 16 * TT)

        @block.gpsimd
        def _(pool):
            pool.memset(ident[:], 0.0).then_inc(s_ident, 1)
            pool.wait_ge(s_ident, 1)
            pool.affine_select(out=ident[:], in_=ident[:], compare_op=ALU.not_equal, fill=1.0, base=0,
                               pattern=[[-1, P]], channel_multiplier=1).then_inc(s_ident, 1)
            pool.memset(mhalf[:], -0.5).then_inc(s_const, 1)

            pool.wait_ge(s_const, 1)
            chain = [0]

            def link(ins):
                chain[0] += 1
                ins.then_inc(s_pchain, 1)
                pool.wait_ge(s_pchain, chain[0])

            def roots(b):
                for t in range(TT):
                    pool.wait_ge(s_ss, 4 * b + 2 * t + 2)
                    link(pool.tensor_tensor(ss[:, 4 + t:5 + t], ss[:, 2 * t:2 * t + 1], ss[:, 2 * t + 1:2 * t + 2],
                                            ALU.add))
                    link(pool.tensor_scalar(ss[:, 6 + t:7 + t], ss[:, 4 + t:5 + t], 1.0 / D, EPS, ALU.mult, ALU.add))
                    pool.tensor_tensor(rstd[:, t:t + 1], ss[:, 6 + t:7 + t], mhalf[:, 0:1], ALU.pow).then_inc(s_rstd, 1)

            def roots_kq(r):
                pool.wait_ge(s_ms, r + 1)
                pool.tensor_tensor(rstd[:, 0:32], ss[:, 32:64], mhalf[:, 0:32], ALU.pow).then_inc(s_rstd, 1)

            def toeplitz(dst, row0, heads):
                src = bass.AP(bias_rows.tensor, row0 * 384 + 1, [[1, P], [384, heads], [1, T]])
                return pool.dma_start(dst, src)

            roots(SQ_NORM[0])
            pool.wait_ge(s_e1, 2)
            pool.dma_start(bias_rows[0:16, :], erow[0:16, 0, :]).then_inc(s_ew, 16)
            pool.wait_ge(s_e2, 1)
            pool.dma_start(bias_rows[16:32, :], erow[0:16, 1, :]).then_inc(s_ew, 16)
            for k in range(KT):
                pool.wait_ge(s_ch, k + 1)
                pool.tensor_tensor(XB[:, k, 1, :], xc[:, k, :], XB[:, k, 0, :].bitcast(F32), ALU.subtract)\
                    .then_inc(s_cl, 1)
            for h in range(2):
                pool.wait_ge(s_lru, 4 * h + 4)
                v = ig[:, 4 * h:4 * h + 4, :]
                pool.tensor_tensor(v, v, xc[:, 4 * h:4 * h + 4, :], ALU.mult).then_inc(s_ix, 1)
            roots(SQ_NORM[1])
            pool.wait_ge(s_ew, 32)
            roots(SQ_NORM[2])
            toeplitz(bias1, 0, 16).then_inc(s_b1l, 16)
            pool.wait_ge(s_b1l, 16)
            pool.memset(bias1[0:CHUNK, :, 0:CHUNK], MASKED).then_inc(s_b1, 1)
            roots(SQ_NORM[3])
            roots_kq(0)
            roots_kq(1)
            pool.wait_ge(s_Sfree, 16)
            toeplitz(bias1, 16, 16).then_inc(s_b2l, 16)
            roots(SQ_NORM[4])
            pool.wait_ge(s_b2l, 16)
            pool.affine_select(out=bias1[:, :, 0:P], in_=bias1[:, :, 0:P], compare_op=ALU.is_ge, fill=MASKED,
                               base=1 - P, pattern=[[0, 16], [1, P]], channel_multiplier=1).then_inc(s_b2, 1)
            pool.affine_select(out=bias1[:, 8:16, P:T], in_=bias1[:, 8:16, P:T], compare_op=ALU.is_ge, fill=MASKED,
                               base=P - 2, pattern=[[0, 8], [-1, P]], channel_multiplier=-1).then_inc(s_b2, 1)
            roots(SQ_NORM[5])
            for b in range(3):
                if b == 2:
                    pool.wait_ge(s_pv, 36)
                    for i, name in enumerate(("norm_mix_post_2", "norm_ffn_post_2")):
                        pool.dma_start(gpost[:, i, :], A[name][0].partition_broadcast(P)).then_inc(s_gp, 16)
                pool.wait_ge(s_sig, b + 1)
                for k in range(8):
                    g = G_BR[b] + k
                    pool.wait_ge(s_evac, g + 1)
                    u = ubr[:, g % 4, :]
                    if b == 0:
                        pool.tensor_tensor(merged[:, k, :], u, g_br[b][:, k, :], ALU.mult).then_inc(s_mdone, 1)
                        continue
                    link(pool.tensor_tensor(u, u, g_br[b][:, k, :], ALU.mult))
                    pool.tensor_tensor(merged[:, k, :], merged[:, k, :], u, ALU.add).then_inc(s_mdone, 1)
            roots(SQ_POST[0])
            roots(SQ_NORM[6])
            roots(SQ_POST[1])

        @block.scalar
        def _(act):
            chain = [0]

            def link(ins):
                chain[0] += 1
                ins.then_inc(s_achain, 1)
                act.wait_ge(s_achain, chain[0])

            def split(u, it=0, units=0, steps=0):
                if u >= N_UNITS:
                    return
                s = u % SLOTS
                act.wait_ge(s_landed[s], it * (16 * units // SLOTS) + LANDED(u))
                if u >= SLOTS:
                    act.wait_ge(s_step, it * steps + AFTER[u - SLOTS])
                if u in U_SWQ:
                    act.activation(swq(whi, s, 0)[0], swq(raw, s, 0)[1], ACT.Copy)
                    act.activation(swq(whi, s, 1)[0], swq(raw, s, 1)[1], ACT.Copy).then_inc(s_hi, 1)
                    return
                act.activation(whi[:, s, :], raw[:, s, :], ACT.Copy).then_inc(s_hi, 1)

            def take(g, step, it=0, groups=0, steps=0, scale=1.0):
                act.wait_ge(s_step, it * steps + step)
                if g >= 4:
                    act.wait_ge(s_evac, it * groups + g - 3)
                act.activation(tmp[:, g % 4, :], PS[:, bank_of(g), T:2 * T], ACT.Copy, scale=scale).then_inc(s_tmp, 1)

            def unit_a(u, g, n=2, scale=1.0):
                split(u + LEAD)
                for m in range(n):
                    take(g + m, BEFORE(u) + m + 1, scale=scale)

            def unit_b(u):
                split(u + LEAD)

            def squares(b, src, ready):
                for i, (t, c, bank) in enumerate(pieces()):
                    ready(i)
                    v = PS[:, bank, :] if src is None else src[:, t, 512 * c:512 * c + 512]
                    if b == SQ_NORM[1]:
                        bank = 5 + 2 * c
                        if t:
                            act.wait_ge(s_ss, 4 * b + c + 1)
                    junk = xn[:, t, 512 * c:512 * c + 512] if src is None else PS[:, bank, :]
                    act.activation(junk, v, ACT.Square, accum_out=ss[:, i:i + 1]).then_inc(s_ss, 1)

            def added(product):
                return lambda i: act.wait_ge(s_add, 4 * product + i + 1)

            def norm(n, src, outs, ready, bank=0):
                squares(SQ_NORM[n], src, ready)
                act.wait_ge(s_xnT, n + 1)
                if n == 0:
                    act.wait_ge(s_vec, 1)
                i = 0
                for X, row in outs:
                    for k in KO:
                        if i >= 2:
                            act.wait_ge(s_xlo, NORM_HI[n] + i - 1)
                        act.activation(X[:, k, 0, :].rearrange("p (t n) -> p t n", t=TT), xnT(bank, k), ACT.Copy,
                                       scale=vecs[:, row + k:row + k + 1]).then_inc(s_xhi, 1)
                        i += 1

            def small(dst, src):
                act.dma_start(dst, src).then_inc(s_small, 16)

            def vec(name, row, n):
                src = A[name].rearrange("a n -> (a n)") if len(A[name].shape) == 2 else A[name]
                small(rows_in[row:row + n, 0, :], src.rearrange("(k n) -> k n", n=P))

            vec("a_norm", R_ANORM, 8)
            vec("kv_norm", R_KV, 8)
            vec("b_norm", R_B, 8)
            vec("mlp_norm", R_MLP, 16)
            vec("norm_mix_pre_2", R_MIX, 8)
            vec("norm_ffn_pre_2", R_FFN, 8)
            vec("norm_mem_2", R_MEM, 8)
            vec("a_conv_b", R_CB, 8)
            small(rows_in[R_CW:R_CW + 32, 0, :], A["a_conv_w"][0].rearrange("w (k n) -> (w k) n", n=P))
            vec("a_lambda", R_LAM, 8)
            small(rows_in[R_BG:R_BG + 16, 0, :], A["a_b_gate"][0].rearrange("b (k n) -> (b k) n", n=P))
            fw = A["ffn_conv_w_2"][0].rearrange("w (k n) -> (w k) n", n=P)
            small(rows_in[0:88, 1, :], fw[0:88])
            small(rows_in[0:44, 2, :], fw[88:132])
            small(rows_in[44:88, 2, :], A["ffn_conv_b_2"][0].rearrange("(k n) -> k n", n=P))
            for r, name in enumerate(("k_norm", "b_q_norm")):
                src = A[name] if r == 0 else A[name][0]
                for half in range(2):
                    small(rows_in[r:r + 1, 3, 64 * half:64 * half + 64], src.rearrange("(a n) -> a n", a=1))
            small(sinks[:], A["swa_sinks_2"][0].partition_broadcast(P))
            small(erow[0:16, 0, 65:65 + NREL], A["b_rel_bias"][0])
            small(relb[0:32, :], A["rel_bias_2"])
            small(onehot[0:32, :], A["bucket_onehot"])

            split(0)
            norm(0, res, [(XA, R_ANORM)], lambda i: act.wait_ge(s_x, 16))
            split(1)
            split(2)
            for i in range(4):
                unit_a(U_REC + i, G_REC + 2 * i)
                for k in range(2 * i, 2 * i + 2):
                    act.wait_ge(s_evac, G_REC + k + 1)
                    act.activation(xc[:, k, :], xrec[:, k, 0:T], ACT.Identity,
                                   scale=vecs[:, R_CW + k:R_CW + k + 1], bias=vecs[:, R_CB + k:R_CB + k + 1])\
                        .then_inc(s_tap, 1)
                for k in range(2 * i, 2 * i + 2):
                    act.wait_ge(s_convd, k + 1)
                    act.activation(XB[:, k, 0, :], xc[:, k, :], ACT.Copy).then_inc(s_ch, 1)
            act.wait_ge(s_sp0, 1)
            act.activation(sp_b[:], sp_a[:], ACT.Exp, scale=-1.0).then_inc(s_spz, 1)
            unit_a(U_GATE[0], G_GATE)
            split(U_LRU + LEAD)
            for n in range(8):
                act.wait_ge(s_step, BEFORE(U_LRU) + n + 1)
                for e, dst in enumerate((rg, ig)):
                    ins = act.activation(dst[:, n, :], PS[:, 4 + n % 4, T * e:T * e + T], ACT.Sigmoid,
                                         bias=vecs[:, R_BG + 2 * n + e:R_BG + 2 * n + e + 1])
                ins.then_inc(s_lru, 1)
            act.wait_ge(s_lru, 8)
            act.wait_ge(s_cc, 1)

            def decays(h):
                for n in range(4 * h, 4 * h + 4):
                    act.activation(av[:, n, :], rg[:, n, :], ACT.Exp, scale=cneg[:, n:n + 1]).then_inc(s_a, 1)
                for n in range(4 * h, 4 * h + 4):
                    act.activation(rg[:, n, :], rg[:, n, :], ACT.Tanh, scale=cpos[:, n:n + 1]).then_inc(s_a, 1)

            unit_a(U_GATE[1], G_GATE + 2)
            decays(0)
            decays(1)
            unit_a(U_GATE[2], G_GATE + 4)
            for h in range(2):
                act.wait_ge(s_q, h + 1)
                act.activation(rg[:, 4 * h:4 * h + 4, :], rg[:, 4 * h:4 * h + 4, :], ACT.Sqrt).then_inc(s_sq, 1)
            unit_a(U_GATE[3], G_GATE + 6)
            act.wait_ge(s_evac, G_GATE + 8)
            for h in range(2):
                act.activation(gate[:, 4 * h:4 * h + 4, :], gate[:, 4 * h:4 * h + 4, :], ACT.Gelu_apprx_tanh)\
                    .then_inc(s_gelu, 1)
            norm(1, xn, [(XB, R_MEM)], lambda i: act.wait_ge(s_mem, 16), bank=4)
            for i in range(2):
                unit_a(U_MEMK + i, G_MEMK + 2 * i)
            for k in range(2):
                act.wait_ge(s_y, k + 1)
                act.activation(XA[:, 4 * k:4 * k + 4, 0, :], xc[:, 4 * k:4 * k + 4, :], ACT.Copy).then_inc(s_yh, 1)
            for i in range(2):
                unit_b(U_MEMV + i)
            for i in range(4):
                unit_b(U_ROUT + i)

            def mlp(layer):
                u0, g0, p0 = mlp_base(layer)
                st0 = BEFORE(u0)

                def hid(j, it=0):
                    act.wait_ge(s_relu, it * 2 + p0 + j + 1)
                    act.activation(XB[:, 2 * (j % 2):2 * (j % 2) + 2, 0, :], up[:, j % 2], ACT.Copy).then_inc(s_hh, 1)

                split(u0 + LEAD)
                take(g0, st0 + 1)
                take(g0 + 1, st0 + 2)
                hid(0)

                def pair_(i, it=0):
                    kw = dict(it=it, units=4, steps=6)
                    split(u0 + 1 + 2 * i + LEAD, **kw)
                    for m in range(2):
                        take(g0 + 2 * i + 2 + m, st0 + 2 + 3 * i + m + 1, it, 4, 6)
                    split(u0 + 2 + 2 * i + LEAD, **kw)
                    hid(i + 1, it)

                with act.Fori(0, 7) as it:
                    pair_(0, it)
                    pair_(1, it)
                pair_(14)
                split(u0 + MLP_UNITS - 1 + LEAD)

            norm(2, res, [(XA, R_MLP)], added(A_ROUT))
            mlp(0)

            norm(3, res, [(XA, R_KV), (XB, R_B)], added(A_MLP0))
            for i in range(4):
                unit_b(U_K + i)

            def kq_square(r):
                act.wait_ge(s_bev, (B_K, B_Q)[r] + 1)
                act.activation(xn, kq, ACT.Square).then_inc(s_kq2, 1)

            def kq_evac(r):
                act.wait_ge(s_kqT, r + 1)
                b0 = 4 if r == 0 else 0
                for b in range(4):
                    act.activation((kT, qT)[r][:, 2 * b:2 * b + 2, :], PS[:, b0 + b, :].rearrange("p (k n) -> p k n", k=2),
                                   ACT.Copy, scale=headg[:, r:r + 1]).then_inc(s_kqev, 1)

            for u0, r in ((U_Q, 0), (U_V, 1)):
                unit_b(u0)
                kq_square(r)
                for i in range(1, 4):
                    unit_b(u0 + i)
                    if i == 2:
                        kq_evac(r)

            def exps(H):
                pr, _, r = place_of(H)
                act.wait_ge(s_max, H + 1)
                if H < 32:
                    act.activation(pr[:, 0:P], pr[:, 0:P], ACT.Exp, bias=snmax[:, r, 0:1],
                                   accum_out=ssum[:, r, 0:1])
                    ins = act.activation(pr[:, P:3 * P], pr[:, P:3 * P], ACT.Exp, bias=snmax[:, r, 1:2],
                                         accum_out=ssum[:, r, 1:2])
                else:
                    act.wait_ge(s_pt, max(H - 1, 32))
                    for t in range(TT):
                        ins = act.activation(pr[:, T * t:T * t + T], PS[:, score_bank(H), T * t:T * t + T], ACT.Exp,
                                             bias=snmax[:, r, t:t + 1], accum_out=ssum[:, r, t:t + 1])
                if 24 <= H < 32:
                    ins = act.activation(ssink[:, r, :], snmax[:, r, :], ACT.Exp, bias=sinks[:, H - 24:H - 23])
                ins.then_inc(s_exp, 1)

            def probs_out(H):
                n = 384 if H < 32 else 512
                act.wait_ge(s_pt, H + 1)
                if H >= 2:
                    act.wait_ge(s_pv, H - 1 if H < 32 else max(H - 1, 32))
                act.activation(place_of(H)[1][:, 0:n], PS[:, 4 + H % 2, 0:n], ACT.Copy).then_inc(s_ptc, 1)

            def attn_hi(H):
                if not ends_out(H):
                    return
                o = out_of(H)
                act.wait_ge(s_pv, H + 1)
                X, k = attn_dst(o)
                if o >= 8:
                    if (o - 8) % 4 == 0 and o >= 16:
                        act.wait_ge(s_step, AFTER[U_BR[0] + 1])
                act.activation(X[:, k, 0, :], PS[:, 6 + o % 2, 0:T], ACT.Copy).then_inc(s_ohi, 1)

            exps(0)
            for H in range(16):
                if H + 1 < 16:
                    exps(H + 1)
                probs_out(H)
                if H:
                    attn_hi(H - 1)
            attn_hi(15)
            for i in range(4):
                unit_b(U_O + i)

            norm(4, res, [(XA, R_MLP + 8)], added(A_O))
            mlp(1)

            norm(5, res, [(XA, R_MIX)], added(A_MLP1))
            for i in range(2):
                unit_a(U_QKV + i, G_QMB + 2 * i, scale=0.125)
            for i in range(2):
                unit_a(U_QKV + 2 + i, G_KMB + 2 * i)
            for i in range(2):
                unit_b(U_QKV + 4 + i)
            for i in range(2):
                unit_a(U_QKV + 6 + i, G_QSW + 2 * i, scale=0.125)
            unit_a(U_QKV + 8, G_KSW, n=1)
            for i in range(2):
                unit_a(U_QKV + 9 + i, G_QME + 2 * i, scale=float(P) ** -0.5)

            def gates(b, k, H, last):
                if H < last:
                    exps(H + 1)
                if k % 2 == 0:
                    split(U_G2[b] + k // 2 + LEAD)
                take(G_G2[b] + k, BEFORE(U_G2[b]) + k + 1)
                if H <= last:
                    probs_out(H)
                if H - 1 <= last and k:
                    attn_hi(H - 1)

            def sigmoid(b):
                act.wait_ge(s_evac, G_G2[b] + 8)
                act.activation(g_br[b], g_br[b], ACT.Sigmoid).then_inc(s_sig, 1)

            exps(16)
            for k in range(8):
                gates(0, k, 16 + k, 31)
            attn_hi(23)
            for k in range(8):
                gates(1, k, 24 + k, 31)
            sigmoid(0)
            sigmoid(1)
            split(U_BR[0] + LEAD)
            take(G_BR[0], BEFORE(U_BR[0]) + 1)
            attn_hi(31)
            for m in range(1, 4):
                take(G_BR[0] + m, BEFORE(U_BR[0]) + m + 1)
            unit_a(U_BR[0] + 1, G_BR[0] + 4, n=4)
            exps(32)
            for k in range(8):
                gates(2, k, 32 + k, 35)
            sigmoid(2)
            for b in (1, 2):
                for i in range(2):
                    unit_a(U_BR[b] + i, G_BR[b] + 4 * i, n=4)
            for k in range(2):
                act.wait_ge(s_mdone, 16 + 4 * (k + 1))
                act.activation(XA[:, 4 * k:4 * k + 4, 0, :], merged[:, 4 * k:4 * k + 4, :], ACT.Copy).then_inc(s_mh, 1)
            for i in range(4):
                unit_b(U_OUT2 + i)

            def product(i_product, u_last):
                return lambda i: act.wait_ge(*((s_tok, 3 * i_product + i + 1) if i < 3 else (s_step, AFTER[u_last])))

            squares(SQ_POST[0], None, product(A_OUT2, U_OUT2 + 3))
            norm(6, res, [(XA, R_FFN)], added(A_OUT2))

            def ffn_act(j):
                act.wait_ge(s_conv2, 2 * j + 1)
                act.activation(fc[:, 0:2, :], fc[:, 0:2, :], ACT.Gelu_apprx_tanh).then_inc(s_gelu2, 1)

            def ffn_hi(j):
                act.wait_ge(s_prod, j + 1)
                act.activation(XB[:, 2 * (j % 2):2 * (j % 2) + 2, 0, :], fc[:, 0:2, :], ACT.Copy).then_inc(s_fh, 1)

            for j in range(FFN_STEPS):
                u = U_FFN if j == 0 else U_FFN + 2 + 3 * (j - 1)
                unit_a(u, G_FFN + 4 * j)
                ffn_act(j)
                unit_a(u + 1, G_FFN + 4 * j + 2)
                ffn_hi(j)
                if j:
                    split(u + 2 + LEAD)
            squares(SQ_POST[1], None, product(A_FFN, N_UNITS - 1))

        @block.tensor
        def _(pe):
            def group(g, slot, m, view, ktiles, X, it=0, groups=0, k0=0, xready=None):
                if g >= ring_of(g):
                    pe.wait_ge(s_evac, it * groups + g - ring_of(g) + 1)
                hi, lo = view(whi, slot), view(wlo, slot)
                lhs = lambda w, k: w[:, k, P * m:P * m + P]
                b = bank_of(g)
                for i, k in enumerate(KO if ktiles == KT else range(ktiles)):
                    if xready is not None:
                        pe.wait_ge(s_xlo, xready + i + 1)
                    both = (PS[:, b, :], lhs(hi, k), X[:, k0 + k, :, :].rearrange("p a n -> p (a n)"))
                    low = (PS[:, b, 0:T], lhs(lo, k), X[:, k0 + k, 0, :])
                    last = i == ktiles - 1
                    if last:
                        pe.matmul(*low, start=False, stop=False, skip_group_check=True)
                        ins = pe.matmul(*both, start=False, stop=True, skip_group_check=True)
                    else:
                        pe.matmul(*both, start=(i == 0), stop=False, skip_group_check=True)
                        pe.matmul(*low, start=False, stop=False, skip_group_check=True)
                ins.then_inc(s_step, 1)

            def have(u, it=0, units=0):
                pe.wait_ge(s_lo, it * units + u + 1)

            def unit_a(u, g, X=XA, xready=None):
                have(u)
                for m in range(2):
                    group(g + m, u % SLOTS, m, W8, KT, X, xready=xready if m == 0 else None)

            def tokens(slot, view, ktiles, X, k0, bank, n, first, last, c0=0, width=512, pieces_=False):
                hi, lo = view(whi, slot), view(wlo, slot)

                def add(t, c, k, part, w, opens, closes):
                    return pe.matmul(PS[:, bank + n * t + c, 0:width], X[:, k0 + k, part, P * t:P * t + P],
                                     w[:, k, c0 + 512 * c:c0 + 512 * c + width], start=opens, stop=closes,
                                     skip_group_check=True)

                if last and pieces_:
                    for t in range(TT):
                        for c in range(n):
                            for k in range(ktiles):
                                for part, w in ((0, hi), (0, lo), (1, hi)):
                                    ins = add(t, c, k, part, w, False, part == 1 and k == ktiles - 1)
                            if (t, c) != (TT - 1, n - 1):
                                ins.then_inc(s_tok, 1)
                    ins.then_inc(s_step, 1)
                    return
                for k in range(ktiles):
                    for t in range(TT):
                        for part, w in ((0, hi), (0, lo), (1, hi)):
                            for c in range(n):
                                ins = add(t, c, k, part, w, first and k == 0 and part == 0 and w is hi,
                                          last and k == ktiles - 1 and part == 1)
                ins.then_inc(s_step, 1)

            def layer_b(u, X, bank=4, pieces_=True, ready=None):
                for i in range(4):
                    have(u + i)
                    if ready is not None:
                        ready(i)
                    tokens((u + i) % SLOTS, W2, 2, X, 2 * i, bank, 2, i == 0, i == 3, pieces_=pieces_)

            def norm_T(n, bank=0):
                for t in range(TT):
                    pe.wait_ge(s_xn, 2 * n + t + 1)
                    for k in range(KT):
                        ins = pe.transpose(PS[:, bank + t + 2 * (k // 4), P * (k % 4):P * (k % 4) + P],
                                           xn[:, t, P * k:P * k + P], ident[:])
                ins.then_inc(s_xnT, 1)

            pe.wait_ge(s_ident, 2)
            norm_T(0)
            pe.wait_ge(s_small, 16 * N_SMALL)
            pe.transpose(PS[:, 4, 0:P], rows_in[:, 0, :], ident[:])
            for r in range(2):
                pe.transpose(PS[:, 4, P + 88 * r:P + 88 * r + 88], rows_in[0:88, 1 + r, :], ident[0:88, 0:88])
            pe.transpose(PS[:, 4, 384:386], rows_in[0:2, 3, :], ident[0:2, 0:2]).then_inc(s_vT, 1)
            pe.matmul(PS[0:16, 5, 0:384], relb[0:32, :], onehot[0:32, :], start=True, stop=True).then_inc(s_eps, 1)
            pe.wait_ge(s_vec, 1)
            pe.wait_ge(s_e2, 1)
            for i in range(4):
                unit_a(U_REC + i, G_REC + 2 * i, xready=NORM_HI[0] if i == 0 else None)
            unit_a(U_GATE[0], G_GATE)
            have(U_LRU)
            s = U_LRU % SLOTS
            for n in range(8):
                pe.wait_ge(s_cl, n + 1)
                if n >= 4:
                    pe.wait_ge(s_lru, n - 3)
                for e in range(2):
                    w, wl = W8(whi, s)[:, n, P * e:P * e + P], W8(wlo, s)[:, n, P * e:P * e + P]
                    dst = PS[:, 4 + n % 4, T * e:T * e + T]
                    pe.matmul(dst, w, XB[:, n, 0, :], start=(e == 0), stop=False, skip_group_check=True)
                    pe.matmul(dst, w, XB[:, n, 1, :], start=False, stop=False, skip_group_check=True)
                    ins = pe.matmul(dst, wl, XB[:, n, 0, :], start=False, stop=(e == 1), skip_group_check=True)
                ins.then_inc(s_step, 1)
            for i in range(1, 4):
                unit_a(U_GATE[i], G_GATE + 2 * i)
            norm_T(1, bank=4)
            for i in range(2):
                unit_a(U_MEMK + i, G_MEMK + 2 * i, X=XB, xready=NORM_HI[1] if i == 0 else None)
            for i in range(2):
                have(U_MEMV + i)
                tokens((U_MEMV + i) % SLOTS, W4, 4, XB, 4 * i, 4, 1, i == 0, i == 1)
            pe.wait_ge(s_bev, B_MEMV + 1)
            layer_b(U_ROUT, XA, ready=lambda i: pe.wait_ge(s_yl, i // 2 + 1))

            def mlp(layer):
                u0, g0, p0 = mlp_base(layer)
                unit_a(u0, g0, xready=NORM_HI[2 if layer == 0 else 4])

                def down(i, j, first=False, last=False, it=0):
                    have(u0 + 2 + 2 * i if not last else u0 + MLP_UNITS - 1, it, 4)
                    pe.wait_ge(s_hl, it * 2 + p0 + j + 1)
                    s = (u0 + 2 + 2 * i if not last else u0 + MLP_UNITS - 1) % SLOTS
                    tokens(s, W2, 2, XB, 2 * (j % 2), 4, 2, first, last, pieces_=True)

                def up_(i, it=0):
                    u = u0 + 1 + 2 * i
                    have(u, it, 4)
                    for m in range(2):
                        group(g0 + 2 * i + 2 + m, u % SLOTS, m, W8, KT, XA, it, 4)

                up_(0)
                down(0, 0, first=True)
                up_(1)
                down(1, 1)
                with pe.Fori(1, 7) as it:
                    up_(0, it)
                    down(0, 0, it=it)
                    up_(1, it)
                    down(1, 1, it=it)
                up_(14)
                down(14, 14)
                down(15, 15, last=True)

            norm_T(2)
            mlp(0)
            norm_T(3)
            layer_b(U_K, XA, pieces_=False, ready=lambda i: pe.wait_ge(s_xlo, NORM_HI[3] + (3, 7, 8, 8)[i]))
            pe.wait_ge(s_xlo, NORM_HI[3] + 16)
            layer_b(U_Q, XB, bank=0, pieces_=False)

            def kq_T(r):
                b0 = 4 if r == 0 else 0
                pe.wait_ge(s_kqn, r + 1)
                for k in range(KT):
                    for t in range(TT):
                        c = T * (k % 2) + P * t
                        ins = pe.transpose(PS[:, b0 + k // 2, c:c + P], kq[:, t, P * k:P * k + P], ident[:])
                ins.then_inc(s_kqT, 1)

            kq_T(0)
            pe.wait_ge(s_kqev, 4)
            layer_b(U_V, XA, pieces_=False)
            kq_T(1)

            def score(H):
                bank = score_bank(H)
                if scored_before(H) > 0 and H < 34:
                    pe.wait_ge(s_Sfree, scored_before(H))
                elif H >= 34:
                    pe.wait_ge(s_exp, H - 1)
                if H < 32:
                    h = H if H < 16 else (H - 16) % 8
                    at, n = ((h % 2), h // 2) if H < 24 else (h // 4, h % 4)
                    q = (qT if H < 16 else qT_mb if H < 24 else qT_sw)[64 * at:64 * at + 64, n, :]
                    k = (kT if H < 16 else kT_mb)[64 * at:64 * at + 64, n, :] if H < 24 else kT_sw[64 * at:64 * at + 64, :]
                    pe.matmul(PS[:, bank, 0:P], q[:, 0:P], k[:, 0:P], start=True, stop=False, skip_group_check=True)
                    ins = pe.matmul(PS[:, bank, P:3 * P], q[:, P:T], k[:, :], start=False, stop=True,
                                    skip_group_check=True)
                else:
                    for t in range(TT):
                        ins = pe.matmul(PS[:, bank, T * t:T * t + T], qT_me[:, H - 32, P * t:P * t + P],
                                        kT_me[:, H - 32, :], start=(t == 0), stop=(t == 1), skip_group_check=True)
                ins.then_inc(s_S, 1)

            CAUSAL = [0, P, 2 * P]
            FULL = [0, 2 * P, P, 3 * P]

            def probs_T(H):
                pe.wait_ge(s_p, H + 1)
                if H >= 2:
                    pe.wait_ge(s_ptc, H - 1)
                at = CAUSAL if H < 32 else FULL
                for i, c in enumerate(at):
                    ins = pe.transpose(PS[:, 4 + H % 2, P * i:P * i + P], place_of(H)[0][:, c:c + P], ident[:])
                ins.then_inc(s_pt, 1)

            def pv(H):
                o = out_of(H)
                pe.wait_ge(s_ptc, H + 1)
                if o >= 2 and (H >= 32 or H % 2 == 0):
                    pe.wait_ge(s_olo, o - 1)
                pT = place_of(H)[1]
                if H < 32:
                    h = H if H < 16 else (H - 16) % 8
                    lo = 64 * (h % 2)
                    v = vtok[:, :, 64 * h:64 * h + 64] if H < 16 else v_mb[:, :, 64 * h:64 * h + 64] if H < 24 \
                        else v_sw[:, :, 64 * (h // 4):64 * (h // 4) + 64]
                    pe.matmul(PS[lo:lo + 64, 6 + o % 2, 0:T], v[:, 0, :], pT[:, 0:T], start=True, stop=False,
                              skip_group_check=True)
                    ins = pe.matmul(PS[lo:lo + 64, 6 + o % 2, P:T], v[:, 1, :], pT[:, T:T + P], start=False,
                                    stop=True, skip_group_check=True)
                else:
                    for j in range(2):
                        ins = pe.matmul(PS[:, 6 + o % 2, 0:T], v_me[:, j, P * (H - 32):P * (H - 32) + P],
                                        pT[:, T * j:T * j + T], start=(j == 0), stop=(j == 1),
                                        skip_group_check=True)
                ins.then_inc(s_pv, 1)

            pe.wait_ge(s_kqev, 8)
            pe.wait_ge(s_bev, B_V + 1)
            score(0)
            score(1)
            for H in range(16):
                if H + 2 < 16:
                    score(H + 2)
                probs_T(H)
                if H:
                    pv(H - 1)
            pv(15)
            pe.wait_ge(s_olo, 8)
            layer_b(U_O, XB)
            norm_T(4)
            mlp(1)
            norm_T(5)
            for i in range(2):
                unit_a(U_QKV + i, G_QMB + 2 * i, xready=NORM_HI[5] if i == 0 else None)
            for i in range(2):
                unit_a(U_QKV + 2 + i, G_KMB + 2 * i)
            for i in range(2):
                have(U_QKV + 4 + i)
                tokens((U_QKV + 4 + i) % SLOTS, W4, 4, XA, 4 * i, 6, 1, i == 0, i == 1)
            for i in range(2):
                unit_a(U_QKV + 6 + i, G_QSW + 2 * i)
            u = U_QKV + 8
            have(u)
            group(G_KSW, u % SLOTS, 0, W8, KT, XA)
            hi, lo = W8(whi, u % SLOTS), W8(wlo, u % SLOTS)
            for t in range(TT):
                for k in range(KT):
                    for part, w in ((0, hi), (0, lo), (1, hi)):
                        ins = pe.matmul(PS[:, 5, P * t:P * t + P], XA[:, k, part, P * t:P * t + P], w[:, k, P:T],
                                        start=(t == 0 and k == 0 and part == 0 and w is hi),
                                        stop=(t == 1 and k == KT - 1 and part == 1), skip_group_check=True)
            ins.then_inc(s_step, 1)
            for i in range(2):
                unit_a(U_QKV + 9 + i, G_QME + 2 * i)
            pe.wait_ge(s_evac, G_QME + 4)
            pe.wait_ge(s_bev, B_VSW + 1)
            def gates(b, k, H, last):
                if H < last:
                    score(H + 1)
                u = U_G2[b] + k // 2
                have(u)
                group(G_G2[b] + k, u % SLOTS, k % 2, W8, KT, XA)
                if H <= last:
                    probs_T(H)
                if H - 1 <= last and k:
                    pv(H - 1)

            def branch(b, k):
                u = U_BR[b] + k // 4
                have(u)
                group(G_BR[b] + k, u % SLOTS, k % 4, W4, 4, XB, k0=4 * (b % 2))

            score(16)
            for k in range(8):
                gates(0, k, 16 + k, 31)
            pv(23)
            for k in range(8):
                gates(1, k, 24 + k, 31)
            pe.wait_ge(s_olo, 12)
            branch(0, 0)
            pv(31)
            for k in range(1, 8):
                branch(0, k)
            score(32)
            for k in range(8):
                gates(2, k, 32 + k, 35)
            pe.wait_ge(s_olo, 20)
            for b in (1, 2):
                for k in range(8):
                    branch(b, k)
            layer_b(U_OUT2, XA, ready=lambda i: pe.wait_ge(s_ml, i // 2 + 1))
            norm_T(6)

            def up2_(j):
                u = U_FFN if j == 0 else U_FFN + 2 + 3 * (j - 1)
                unit_a(u, G_FFN + 4 * j, xready=NORM_HI[6] if j == 0 else None)
                unit_a(u + 1, G_FFN + 4 * j + 2)

            def down2(j):
                u = U_FFN + 4 + 3 * j if j < FFN_STEPS - 1 else N_UNITS - 1
                have(u)
                pe.wait_ge(s_fl, j + 1)
                tokens(u % SLOTS, W2, 2, XB, 2 * (j % 2), 4, 2, j == 0, j == FFN_STEPS - 1, pieces_=True)

            up2_(0)
            for j in range(FFN_STEPS - 1):
                up2_(j + 1)
                down2(j)
            down2(FFN_STEPS - 1)

        @block.vector
        def _(dve):
            chain = [0]

            def link(ins):
                chain[0] += 1
                ins.then_inc(s_chain, 1)
                dve.wait_ge(s_chain, chain[0])

            def split(u, it=0, units=0):
                if u >= N_UNITS:
                    return
                s = u % SLOTS
                dve.wait_ge(s_hi, it * units + u + 1)
                if u in U_SWQ:
                    for j in range(2):
                        ins = dve.tensor_tensor(swq(wlo, s, j)[0], swq(raw, s, j)[1], swq(whi, s, j)[0].bitcast(F32),
                                                ALU.subtract)
                    ins.then_inc(s_lo, 1)
                    return
                dve.tensor_tensor(wlo[:, s, :], raw[:, s, :], whi[:, s, :].bitcast(F32), ALU.subtract).then_inc(s_lo, 1)

            def join(g, dst, it=0, groups=0, scale=1.0):
                dve.wait_ge(s_tmp, it * groups + g + 1)
                b = bank_of(g)
                if scale == 1.0:
                    dve.tensor_tensor(dst, PS[:, b, 0:T], tmp[:, g % 4, :], ALU.add).then_inc(s_evac, 1)
                else:
                    dve.scalar_tensor_tensor(dst, PS[:, b, 0:T], scale, tmp[:, g % 4, :], ALU.mult,
                                             ALU.add).then_inc(s_evac, 1)

            def unit_a(u, g, dsts, scale=1.0):
                split(u + LEAD)
                for m, dst in enumerate(dsts):
                    join(g + m, dst, scale=scale)

            def norm(n, src, outs, bank=0):
                for t in range(TT):
                    dve.wait_ge(s_rstd, ROOTS[SQ_NORM[n]] + t + 1)
                    dve.tensor_scalar(xn[:, t, :], src[:, t, :], rstd[:, t:t + 1], None, ALU.mult).then_inc(s_xn, 1)
                norm_lo(n, outs, bank)

            def norm_lo(n, outs, bank=0):
                i = NORM_HI[n]
                for X, row in outs:
                    for k in KO:
                        i += 1
                        dve.wait_ge(s_xhi, i)
                        hi, lo = (X[:, k, j, :].rearrange("p (t n) -> p t n", t=TT) for j in range(2))
                        dve.scalar_tensor_tensor(lo, xnT(bank, k), vecs[:, row + k:row + k + 1], hi.bitcast(F32),
                                                 ALU.mult, ALU.subtract).then_inc(s_xlo, 1)

            def add_out(product, u_last):
                for i, (t, c, bank) in enumerate(pieces()):
                    dve.wait_ge(*((s_tok, 3 * product + i + 1) if i < 3 else (s_step, AFTER[u_last])))
                    v = res[:, t, 512 * c:512 * c + 512]
                    dve.tensor_tensor(v, v, PS[:, bank, :], ALU.add).then_inc(s_add, 1)

            dve.memset(xrec[:, :, 0:3], 0.0)
            for t in range(TT):
                dve.wait_ge(s_rstd, t + 1)
                dve.tensor_scalar(xn[:, t, :], res[:, t, :], rstd[:, t:t + 1], None, ALU.mult).then_inc(s_xn, 1)
            dve.wait_ge(s_vT, 1)
            link(dve.tensor_copy(vecs[:], PS[:, 4, 0:P]))
            dve.tensor_copy(fvec[:, :, :], PS[:, 4, P:P + 176].rearrange("p (a b) -> p a b", a=2))
            dve.tensor_copy(headg[:, 0:1], PS[:, 4, 384:385])
            dve.tensor_scalar(headg[:, 1:2], PS[:, 4, 385:386], 0.125, None, ALU.mult).then_inc(s_vec, 1)
            split(0)
            norm_lo(0, [(XA, R_ANORM)])
            split(1)
            split(2)
            dve.wait_ge(s_small, 16 * N_SMALL)
            dve.tensor_copy(erow[0:16, 0, 0:65], erow[0:16, 0, 65:66].to_broadcast([16, 65])).then_inc(s_e1, 1)
            dve.tensor_copy(erow[0:16, 0, 65 + NREL:384],
                            erow[0:16, 0, 64 + NREL:65 + NREL].to_broadcast([16, 384 - 65 - NREL])).then_inc(s_e1, 1)
            dve.wait_ge(s_eps, 1)
            dve.tensor_copy(erow[0:16, 1, :], PS[0:16, 5, 0:384]).then_inc(s_e2, 1)
            lam = vecs[:, R_LAM:R_LAM + 8]
            link(dve.tensor_scalar(sp_c[:], lam, -1.0, None, ALU.mult))
            dve.tensor_tensor(sp_a[:], lam, sp_c[:], ALU.max).then_inc(s_sp0, 1)
            link(dve.tensor_scalar(sp_c[:], sp_c[:], 0.0, None, ALU.max))

            def softplus():
                dve.wait_ge(s_spz, 1)
                link(dve.tensor_scalar(sp_a[:], sp_b[:], 2.0, None, ALU.add))
                link(dve.reciprocal(sp_a[:], sp_a[:]))
                link(dve.tensor_tensor(sp_b[:], sp_b[:], sp_a[:], ALU.mult))
                link(dve.tensor_tensor(sp_a[:], sp_b[:], sp_b[:], ALU.mult))
                TERMS = 9
                link(dve.tensor_scalar(cneg[:], sp_a[:], 2.0 / (2 * TERMS + 1), 2.0 / (2 * TERMS - 1), ALU.mult, ALU.add))
                for n in range(TERMS - 2, -1, -1):
                    link(dve.tensor_tensor(cneg[:], cneg[:], sp_a[:], ALU.mult))
                    link(dve.tensor_scalar(cneg[:], cneg[:], 2.0 / (2 * n + 1), None, ALU.add))
                link(dve.tensor_tensor(cneg[:], cneg[:], sp_b[:], ALU.mult))
                link(dve.tensor_tensor(cneg[:], cneg[:], sp_c[:], ALU.add))
                link(dve.tensor_scalar(cpos[:], cneg[:], LRU_C, None, ALU.mult))
                dve.tensor_scalar(cneg[:], cneg[:], -LRU_C, None, ALU.mult).then_inc(s_cc, 1)

            def conv(k0):
                for i in range(1, 4):
                    for k in (k0, k0 + 1):
                        if i == 1:
                            dve.wait_ge(s_tap, k + 1)
                        ins = dve.scalar_tensor_tensor(xc[:, k, :], xrec[:, k, i:i + T],
                                                       vecs[:, R_CW + 8 * i + k:R_CW + 8 * i + k + 1], xc[:, k, :],
                                                       ALU.mult, ALU.add)
                        if i == 3:
                            ins.then_inc(s_convd, 1)
                    if i < 3:
                        link(ins)

            for i in range(4):
                unit_a(U_REC + i, G_REC + 2 * i, [xrec[:, 2 * i + m, 3:3 + T] for m in range(2)])
                conv(2 * i)
            softplus()
            dve.wait_ge(s_ew, 32)

            def gate_unit(i):
                unit_a(U_GATE[i], G_GATE + 2 * i, [gate[:, 2 * i + m, :] for m in range(2)])

            def half(v, h):
                return v[:, 4 * h:4 * h + 4, :].rearrange("p a b -> p (a b)")

            gate_unit(0)
            split(U_LRU + LEAD)
            gate_unit(1)
            for h in range(2):
                dve.wait_ge(s_a, 8 * h + 4)
                link(dve.tensor_tensor(half(sq, h), half(av, h), half(av, h), ALU.mult))
                dve.wait_ge(s_a, 8 * h + 8)
                dve.scalar_tensor_tensor(half(rg, h), half(sq, h), 1.0, half(rg, h), ALU.add, ALU.mult).then_inc(s_q, 1)
            gate_unit(2)
            gate_unit(3)
            for h in range(2):
                dve.wait_ge(s_sq, h + 1)
                dve.wait_ge(s_ix, h + 1)
                link(dve.tensor_tensor(half(ig, h), half(ig, h), half(rg, h), ALU.mult))
                for k in range(4 * h, 4 * h + 4):
                    ins = dve.tensor_tensor_scan(rg[:, k, :], av[:, k, :], ig[:, k, :], 0.0, ALU.mult, ALU.add)
                link(ins)
            norm(1, xn, [(XB, R_MEM)], bank=4)
            for h in range(2):
                dve.wait_ge(s_gelu, h + 1)
                dve.tensor_tensor(half(xc, h), half(rg, h), half(gate, h), ALU.mult).then_inc(s_y, 1)
            for i in range(2):
                unit_a(U_MEMK + i, G_MEMK + 2 * i, [kT_me[:, 2 * i + m, :] for m in range(2)])
            for k in range(2):
                dve.wait_ge(s_yh, k + 1)
                dve.tensor_tensor(XA[:, 4 * k:4 * k + 4, 1, :], xc[:, 4 * k:4 * k + 4, :],
                                  XA[:, 4 * k:4 * k + 4, 0, :].bitcast(F32), ALU.subtract).then_inc(s_yl, 1)
            for i in range(2):
                split(U_MEMV + i + LEAD)
            dve.wait_ge(s_step, AFTER[U_MEMV + 1])
            dve.tensor_copy(v_me[:], PS[:, 4:6, :]).then_inc(s_bev, 1)
            for i in range(4):
                split(U_ROUT + i + LEAD)
            add_out(A_ROUT, U_ROUT + 3)

            def mlp(layer):
                u0, g0, p0 = mlp_base(layer)

                def relu2(j, it=0):
                    dve.wait_ge(s_evac, it * 4 + g0 + 2 * j + 2)
                    v = up[:, j % 2].rearrange("p a b -> p (a b)")
                    dve.scalar_tensor_tensor(v, v, 0.0, v, ALU.max, ALU.mult).then_inc(s_relu, 1)

                def hid_lo(j, it=0):
                    dve.wait_ge(s_hh, it * 2 + p0 + j + 1)
                    k = 2 * (j % 2)
                    dve.tensor_tensor(XB[:, k:k + 2, 1, :], up[:, j % 2], XB[:, k:k + 2, 0, :].bitcast(F32),
                                      ALU.subtract).then_inc(s_hl, 1)

                def pair_(i, it=0):
                    split(u0 + 1 + 2 * i + LEAD, it, 4)
                    for m in range(2):
                        join(g0 + 2 * i + 2 + m, up[:, (i + 1) % 2, m, :], it, 4)
                    relu2(i + 1, it)
                    split(u0 + 2 + 2 * i + LEAD, it, 4)
                    hid_lo(i + 1, it)

                split(u0 + LEAD)
                join(g0, up[:, 0, 0, :])
                join(g0 + 1, up[:, 0, 1, :])
                relu2(0)
                hid_lo(0)
                with dve.Fori(0, 7) as it:
                    pair_(0, it)
                    pair_(1, it)
                pair_(14)
                split(u0 + MLP_UNITS - 1 + LEAD)
                add_out((A_MLP0, A_MLP1)[layer], u0 + MLP_UNITS - 1)

            norm(2, res, [(XA, R_MLP)])
            mlp(0)

            norm(3, res, [(XA, R_KV), (XB, R_B)])
            for i in range(4):
                split(U_K + i + LEAD)

            def kq_out(r, u_last, bank):
                dve.wait_ge(s_step, AFTER[u_last])
                if r:
                    dve.wait_ge(s_kqT, 1)
                for t in range(TT):
                    ins = dve.tensor_copy(kq[:, t, :], PS[:, bank + 2 * t:bank + 2 * t + 2, :].rearrange("p a b -> p (a b)"))
                ins.then_inc(s_bev, 1)

            def kq_norm(r):
                dve.wait_ge(s_kq2, r + 1)
                link(dve.tensor_reduce(ss[:, 0:32], xn.rearrange("p t (h d) -> p (t h) d", d=64), AX_X, ALU.add))
                ins = dve.tensor_scalar(ss[:, 32:64], ss[:, 0:32], 1.0 / 64, EPS, ALU.mult, ALU.add)
                ins.then_inc(s_ms, 1)
                dve.wait_ge(s_rstd, ROOTS_KQ[r] + 1)
                v = kq.rearrange("p t (h d) -> p (t h) d", d=64)
                dve.tensor_tensor(v, v, rstd[:, 0:32].unsqueeze(2).to_broadcast([P, 32, 64]), ALU.mult)\
                   .then_inc(s_kqn, 1)

            split(U_Q + LEAD)
            kq_out(0, U_K + 3, 4)
            kq_norm(0)
            for i in range(1, 4):
                split(U_Q + i + LEAD)
            split(U_V + LEAD)
            kq_out(1, U_Q + 3, 0)
            kq_norm(1)
            for i in range(1, 4):
                split(U_V + i + LEAD)
            dve.wait_ge(s_step, AFTER[U_V + 3])
            for t in range(TT):
                ins = dve.tensor_copy(vtok[:, t, :], PS[:, 4 + 2 * t:6 + 2 * t, :].rearrange("p a b -> p (a b)"))
            ins.then_inc(s_bev, 1)

            def row_max(H):
                pr, _, r = place_of(H)
                bank = score_bank(H)
                dve.wait_ge(s_S, H + 1)
                if H < 32:
                    if H >= 3:
                        dve.wait_ge(s_pt, H - 2)
                    h = H if H < 16 else H - 16
                    own, both = bias1[:, h, P - 1::-1], bias1[:, h, ::-1]
                    dve.tensor_tensor_reduce(pr[:, 0:P], PS[:, bank, 0:P], own, 1.0, -3.0e38, ALU.add,
                                             ALU.max, smax[:, r, 0:1])
                    ins = dve.tensor_tensor_reduce(pr[:, P:3 * P], PS[:, bank, P:3 * P], both, 1.0, -3.0e38,
                                                   ALU.add, ALU.max, smax[:, r, 1:2])
                    ins.then_inc(s_Sfree, 1)
                    dve.wait_ge(s_Sfree, H + 1)
                else:
                    link(dve.tensor_reduce(smax[:, r, :], PS[:, bank, :].rearrange("p (t n) -> p t n", t=TT), AX_X,
                                           ALU.max))
                if 24 <= H < 32:
                    link(dve.tensor_scalar(smax[:, r, :], smax[:, r, :], sinks[:, H - 24:H - 23], None, ALU.max))
                dve.tensor_scalar(snmax[:, r, :], smax[:, r, :], -1.0, None, ALU.mult).then_inc(s_max, 1)

            def norm_probs(H):
                pr, _, r = place_of(H)
                dve.wait_ge(s_exp, H + 1)
                if 24 <= H < 32:
                    link(dve.tensor_tensor(ssum[:, r, :], ssum[:, r, :], ssink[:, r, :], ALU.add))
                link(dve.reciprocal(srec[:, r, :], ssum[:, r, :]))
                w = P if H < 32 else T
                dve.tensor_scalar(pr[:, 0:w], pr[:, 0:w], srec[:, r, 0:1], None, ALU.mult)
                dve.tensor_scalar(pr[:, w:w + T], pr[:, w:w + T], srec[:, r, 1:2], None, ALU.mult).then_inc(s_p, 1)

            def attn_lo(H):
                if not ends_out(H):
                    return
                o = out_of(H)
                dve.wait_ge(s_ohi, o + 1)
                X, k = attn_dst(o)
                dve.tensor_tensor(X[:, k, 1, :], PS[:, 6 + o % 2, 0:T], X[:, k, 0, :].bitcast(F32), ALU.subtract)\
                   .then_inc(s_olo, 1)

            dve.wait_ge(s_b1, 1)
            row_max(0)
            for H in range(16):
                if H + 1 < 16:
                    row_max(H + 1)
                norm_probs(H)
                if H:
                    attn_lo(H - 1)
            attn_lo(15)
            for i in range(4):
                split(U_O + i + LEAD)
            add_out(A_O, U_O + 3)
            norm(4, res, [(XA, R_MLP + 8)])
            mlp(1)

            norm(5, res, [(XA, R_MIX)])
            for i in range(2):
                unit_a(U_QKV + i, G_QMB + 2 * i, [qT_mb[:, 2 * i + m, :] for m in range(2)], scale=0.125)
            for i in range(2):
                unit_a(U_QKV + 2 + i, G_KMB + 2 * i, [kT_mb[:, 2 * i + m, :] for m in range(2)])
            for i in range(2):
                split(U_QKV + 4 + i + LEAD)
            dve.wait_ge(s_step, AFTER[U_QKV + 5])
            dve.tensor_copy(v_mb, PS[:, 6:8, :]).then_inc(s_bev, 1)
            for i in range(2):
                unit_a(U_QKV + 6 + i, G_QSW + 2 * i, [qT_sw[:, 2 * i + m, :] for m in range(2)], scale=0.125)
            unit_a(U_QKV + 8, G_KSW, [kT_sw])
            dve.wait_ge(s_step, AFTER[U_QKV + 8])
            dve.tensor_copy(v_sw, PS[:, 5, 0:T].rearrange("p (t n) -> p t n", t=TT)).then_inc(s_bev, 1)
            for i in range(2):
                unit_a(U_QKV + 9 + i, G_QME + 2 * i, [qT_me[:, 2 * i + m, :] for m in range(2)],
                       scale=float(P) ** -0.5)
            dve.wait_ge(s_b2, 2)
            def gates(b, k, H, last):
                if H < last:
                    row_max(H + 1)
                if H <= last:
                    norm_probs(H)
                if k % 2 == 0:
                    split(U_G2[b] + k // 2 + LEAD)
                if b == 2:
                    dve.wait_ge(s_mdone, k + 1)
                join(G_G2[b] + k, g_br[b][:, k, :])
                if H - 1 <= last and k:
                    attn_lo(H - 1)

            def branch(b, k):
                g = G_BR[b] + k
                if 8 * b + k >= 4:
                    dve.wait_ge(s_mdone, 8 * b + k - 3)
                join(g, ubr[:, g % 4, :])

            row_max(16)
            for k in range(8):
                gates(0, k, 16 + k, 31)
            attn_lo(23)
            for k in range(8):
                gates(1, k, 24 + k, 31)
            split(U_BR[0] + LEAD)
            branch(0, 0)
            attn_lo(31)
            for k in range(1, 8):
                if k == 4:
                    split(U_BR[0] + 1 + LEAD)
                branch(0, k)
            row_max(32)
            for k in range(8):
                gates(2, k, 32 + k, 35)
            for b in (1, 2):
                for k in range(8):
                    if k % 4 == 0:
                        split(U_BR[b] + k // 4 + LEAD)
                    branch(b, k)
            for k in range(2):
                dve.wait_ge(s_mh, k + 1)
                dve.tensor_tensor(XA[:, 4 * k:4 * k + 4, 1, :], merged[:, 4 * k:4 * k + 4, :],
                                  XA[:, 4 * k:4 * k + 4, 0, :].bitcast(F32), ALU.subtract).then_inc(s_ml, 1)
            for i in range(4):
                split(U_OUT2 + i + LEAD)

            def post(n):
                dve.wait_ge(s_gp, 32)
                for t in range(TT):
                    dve.wait_ge(s_rstd, ROOTS[SQ_POST[n]] + t + 1)
                    link(dve.scalar_tensor_tensor(xn[:, t, :], PS[:, 4 + 2 * t:6 + 2 * t, :].rearrange("p a b -> p (a b)"),
                                                  rstd[:, t:t + 1], gpost[:, n, :], ALU.mult, ALU.mult))
                    for c in range(2):
                        v = res[:, t, 512 * c:512 * c + 512]
                        dve.tensor_tensor(v, v, xn[:, t, 512 * c:512 * c + 512], ALU.add).then_inc(s_add, 1)

            post(0)
            norm(6, res, [(XA, R_FFN)])
            for k in range(4):
                ins = dve.memset(fu[:, k, 0:2], 0.0)
            link(ins)

            def conv2(g0, e, j):
                tiles = [(e * 22 + 2 * j + m, 2 * e + m) for m in range(2)]
                for m, (c, f) in enumerate(tiles):
                    join(g0 + m, fu[:, f, 2:2 + T])
                for m, (c, f) in enumerate(tiles):
                    dve.wait_ge(s_evac, g0 + m + 1)
                    ins = dve.tensor_scalar(fc[:, f, :], fu[:, f, 0:T], fvec[:, 0, c:c + 1], fvec[:, 1, 44 + c:45 + c],
                                            ALU.mult, ALU.add)
                link(ins)
                for i, w in ((1, fvec[:, 0, 44:88]), (2, fvec[:, 1, 0:44])):
                    for c, f in tiles:
                        ins = dve.scalar_tensor_tensor(fc[:, f, :], fu[:, f, i:i + T], w[:, c:c + 1], fc[:, f, :],
                                                       ALU.mult, ALU.add)
                    if i == 1:
                        link(ins)
                return ins

            for j in range(FFN_STEPS):
                u = U_FFN if j == 0 else U_FFN + 2 + 3 * (j - 1)
                for e in range(2):
                    split(u + e + LEAD)
                    if e == 0 and j:
                        dve.wait_ge(s_fh, j)
                    conv2(G_FFN + 4 * j + 2 * e, e, j).then_inc(s_conv2, 1)
                dve.wait_ge(s_conv2, 2 * j + 2)
                dve.wait_ge(s_gelu2, j + 1)
                dve.tensor_tensor(fc[:, 0:2, :], fc[:, 0:2, :], fc[:, 2:4, :], ALU.mult).then_inc(s_prod, 1)
                k = 2 * (j % 2)
                dve.wait_ge(s_fh, j + 1)
                dve.tensor_tensor(XB[:, k:k + 2, 1, :], fc[:, 0:2, :], XB[:, k:k + 2, 0, :].bitcast(F32),
                                  ALU.subtract).then_inc(s_fl, 1)
                if j:
                    split(u + 2 + LEAD)
            post(1)



def bucket_onehot():
    n = np.maximum(np.arange(384) - P, 0)
    nf = np.maximum(n, 1).astype(np.float32)
    large = 16 + (np.log(nf / np.float32(16)) / np.float32(np.log(128 / 16)) * np.float32(16)).astype(np.int32)
    bucket = np.where(n < 16, n, np.minimum(large, 31))
    return (bucket[None, :] == np.arange(32)[:, None]).astype(np.float32)


_INS = ['x', 'a_norm', 'a_w_in', 'a_conv_w', 'a_conv_b', 'a_w_gate', 'a_b_gate', 'a_lambda', 'a_w_out', 'kv_norm',
        'w_kv', 'k_norm', 'b_norm', 'b_w_q', 'b_q_norm', 'b_rel_bias', 'b_w_o', 'mlp_norm', 'w_up', 'w_down', 'mem_2',
        'norm_mix_pre_2', 'norm_mix_post_2', 'norm_ffn_pre_2', 'norm_ffn_post_2', 'norm_mem_2', 'w_in_2', 'rel_bias_2',
        'swa_sinks_2', 'w_mem_kv_2', 'w_branch_moba_2', 'w_branch_swa_2', 'w_branch_mem_2', 'w_out_2', 'w_ffn_up_2',
        'ffn_conv_w_2', 'ffn_conv_b_2', 'w_ffn_down_2']


def kernel(**inputs):
    import numpy as _np
    import concourse.bacc as _bacc
    from concourse import mybir as _mybir
    from concourse.bass_utils import run_bass_kernel_spmd as _run

    nc = _bacc.Bacc("TRN2", target_bir_lowering=False, num_devices=1)
    arrays, A = {}, {}
    for name in _INS + ['bucket_onehot']:
        a = bucket_onehot() if name == 'bucket_onehot' else _np.asarray(inputs[name])
        a = _np.ascontiguousarray(a)
        arrays[f"in_{name}"] = a
        A[name] = nc.dram_tensor(f"in_{name}", a.shape, _mybir.dt.from_np(a.dtype), kind="ExternalInput").ap()
    out = nc.dram_tensor("out_0", (1, 256, 1024), _mybir.dt.float32, kind="ExternalOutput").ap()
    bass_blocks(nc, A, out)
    r = _run(nc, [arrays], core_ids=[0])
    return r.results[0]["out_0"]
```

```python
from contextlib import ExitStack

import numpy as np

import concourse.bass as bass
from concourse import mybir

F32 = mybir.dt.float32
F32R = mybir.dt.float32r
ALU = mybir.AluOpType
ACT = mybir.ActivationFunctionType
AX_X = mybir.AxisListType.X

P = 128
T = 256
TT = T // P
D = 1024
KT = D // P
EPS = 1e-6
D_FF = 4096
FFN = 2816
CHUNK = 64
NREL = 192
MASKED = -1.0e30
LRU_C = 8.0
SLOTS = 4
LEAD = 3
UNIT = 2048

U_REC, U_GATE, U_LRU = [0, 1, 3, 5], [2, 4, 6, 7], 8
U_MEMK, U_MEMV, U_ROUT = 9, 11, 13
U_MLP0 = 17
U_K, U_Q, U_V, U_O = 49, 53, 57, 61
U_MLP1 = 65
U_QKV = 97
U_G2 = [108, 112, 118]
U_BR = [116, 122, 124]
U_SWQ = (103, 104)
U_OUT2 = 126
U_FFN = 130
N_UNITS = 163
MLP_UNITS = 2 * D_FF // 256
FFN_STEPS = FFN // 256

G_REC, G_GATE, G_MEMK = [0, 2, 6, 10], [4, 8, 12, 14], 16
G_MLP0, G_MLP1 = 20, 52
G_QMB, G_KMB, G_QSW, G_KSW, G_QME = 84, 88, 92, 96, 97
G_G2 = [101, 109, 125]
G_BR = [117, 133, 141]
G_FFN = 149


def steps_of_units():
    n = []
    for u in range(N_UNITS):
        if u == U_LRU:
            n.append(8)
        elif u < U_MEMV:
            n.append(2)
        elif U_MLP0 <= u < U_K or U_MLP1 <= u < U_QKV:
            v = u - (U_MLP0 if u < U_K else U_MLP1)
            n.append(2 if v == 0 or (v % 2 and v < MLP_UNITS - 1) else 1)
        elif U_QKV <= u < U_G2[0]:
            n.append([2, 2, 2, 2, 1, 1, 2, 2, 2, 2, 2][u - U_QKV])
        elif U_G2[0] <= u < U_OUT2:
            n.append(4 if any(v <= u < v + 2 for v in U_BR) else 2)
        elif u >= U_FFN:
            v = u - U_FFN
            n.append(2 if v < 2 or (v < N_UNITS - U_FFN - 1 and (v - 2) % 3 < 2) else 1)
        else:
            n.append(1)
    return n


STEPS = steps_of_units()
AFTER = [sum(STEPS[:u + 1]) for u in range(N_UNITS)]


def LANDED(u):
    return 16 * (u // SLOTS + 1) + 16 * sum(v <= u and v % SLOTS == u % SLOTS for v in U_SWQ)


def BEFORE(u):
    return sum(STEPS[:u])


B_MEMV, B_K, B_Q, B_V0, B_V, B_VMB, B_VSW = range(7)
A_ROUT, A_MLP0, A_O, A_MLP1, A_OUT2, A_FFN = range(6)
SQ_NORM = [0, 1, 2, 3, 4, 5, 7]
SQ_POST = [6, 8]
ROOTS = [2 * i for i in range(9)]
KO = [0, 4, 1, 5, 2, 6, 3, 7]


def bank_of(g):
    if g in [f + i for f in (G_REC[0], G_MLP0, G_MLP1, G_QMB, G_FFN) for i in range(2)]:
        return 4 + g % 2
    for b in G_BR:
        if b <= g < b + 8:
            return (1, 0, 2, 3)[(g - b) % 4]
    return g % 2 if G_G2[0] <= g < G_FFN else g % 4


def ring_of(g):
    if g in (G_BR[0], G_BR[0] + 1, G_BR[1], G_BR[1] + 1):
        return 2
    return 2 if any(b <= g < b + 8 for b in G_G2) else 4


R_ANORM, R_KV, R_B, R_MLP, R_MIX, R_FFN, R_MEM, R_CB, R_CW, R_LAM, R_BG = 0, 8, 16, 24, 40, 48, 56, 64, 72, 104, 112


def bass_blocks(nc, A, out):
    w_units = []

    def cols(w, k, c0):
        return w[:, c0:c0 + 256].rearrange("(k p) n -> p k n", p=P)

    def rows(w, r0, n=2, c0=0, nn=D):
        return w[r0:r0 + n * P, c0:c0 + nn].rearrange("(k p) n -> p k n", p=P)

    a_in = A["a_w_in"][0]
    w_in2 = A["w_in_2"][0]
    w_kv = A["w_kv"]
    w_mem = A["w_mem_kv_2"][0]
    rec = [cols(a_in, KT, D + 256 * i) for i in range(4)]
    gate_ = [cols(a_in, KT, 256 * i) for i in range(4)]
    w_units += [rec[0], rec[1], gate_[0], rec[2], gate_[1], rec[3], gate_[2]]
    w_units += [gate_[3], A["a_w_gate"][0].rearrange("k p n -> p k n")]
    w_units += [cols(w_mem, KT, 256 * i) for i in range(2)]
    w_units += [rows(w_mem, 512 * i, 4, 512, 512) for i in range(2)]
    w_units += [rows(A["a_w_out"][0], 256 * i) for i in range(4)]

    def mlp_units(layer):
        up = [cols(A["w_up"][layer], KT, 256 * i) for i in range(16)]
        down = [rows(A["w_down"][layer], 256 * i) for i in range(16)]
        us = [up[0]]
        for i in range(15):
            us += [up[i + 1], down[i]]
        return us + [down[15]]

    w_units += mlp_units(0)
    w_units += [rows(w_kv, 256 * i) for i in range(4)]
    w_units += [rows(A["b_w_q"][0], 256 * i) for i in range(4)]
    w_units += [rows(w_kv, 256 * i, 2, D, D) for i in range(4)]
    w_units += [rows(A["b_w_o"][0], 256 * i) for i in range(4)]
    w_units += mlp_units(1)
    w_units += [cols(w_in2, KT, 256 * i) for i in range(4)]
    w_units += [rows(w_in2, 512 * i, 4, 1024, 512) for i in range(2)]
    w_units += [w_in2[:, 1536:2048].rearrange("(k p) (h n) -> p k h n", p=P, h=2)[:, :, :, P * i:P * i + P]
                for i in range(2)]
    w_units += [cols(w_in2, KT, 2048 + 256 * i) for i in range(3)]
    gates2 = lambda b: [cols(w_in2, KT, 2816 + D * b + 256 * i) for i in range(4)]
    branch = lambda name: [rows(A[name][0], 0, 4, 512 * i, 512) for i in range(2)]
    w_units += gates2(0) + gates2(1) + branch("w_branch_moba_2") + gates2(2)
    w_units += branch("w_branch_swa_2") + branch("w_branch_mem_2")
    w_units += [rows(A["w_out_2"][0], 256 * i) for i in range(4)]
    up2, down2 = A["w_ffn_up_2"][0], A["w_ffn_down_2"][0]
    pair = lambda j: [cols(up2, KT, 256 * j), cols(up2, KT, FFN + 256 * j)]
    w_units += pair(0)
    for j in range(FFN_STEPS - 1):
        w_units += pair(j + 1) + [rows(down2, 256 * j)]
    w_units += [rows(down2, 256 * (FFN_STEPS - 1))]
    assert len(w_units) == N_UNITS

    ctx = ExitStack()
    with ctx:
        def sb(name, shape, dt=F32):
            return ctx.enter_context(nc.sbuf_tensor(name, shape, dt))

        def sem(name):
            return ctx.enter_context(nc.semaphore(name))

        bias_rows = nc.dram_tensor("bias_rows", [32, 384], F32, kind="Internal").ap()

        raw = sb("raw", [P, SLOTS, UNIT])
        whi = sb("whi", [P, SLOTS, UNIT], F32R)
        wlo = sb("wlo", [P, SLOTS, UNIT], F32R)
        res = sb("res", [P, TT, D])
        XA = sb("XA", [P, KT, 2, T], F32R)
        XB = sb("XB", [P, KT, 2, T], F32R)
        kT_me = sb("kT_me", [P, 4, T])
        v_me = sb("v_me", [P, TT, 512])
        arena = sb("arena", [P, 5 * 2048 + 2072 + 2048])
        ident = sb("ident", [P, P])
        vecs = sb("vecs", [P, P])
        fvec = sb("fvec", [P, 2, 88])
        headg = sb("headg", [P, 2])
        sinks = sb("sinks", [P, 8])
        sp_a = sb("sp_a", [P, 8])
        sp_b = sb("sp_b", [P, 8])
        sp_c = sb("sp_c", [P, 8])
        cneg = sb("cneg", [P, 8])
        cpos = sb("cpos", [P, 8])
        ss = sb("ss", [P, 64])
        rstd = sb("rstd", [P, 32])
        mhalf = sb("mhalf", [P, 32])
        smax = sb("smax", [P, 3, 2])
        snmax = sb("snmax", [P, 3, 2])
        ssum = sb("ssum", [P, 3, 2])
        ssink = sb("ssink", [P, 3, 2])
        srec = sb("srec", [P, 3, 2])
        PS = ctx.enter_context(nc.psum_tensor("PS", [P, 8, 512], F32))

        def area(o, n):
            return arena[:, o:o + n]

        S = [2048 * i for i in range(5)]
        XRO = 5 * 2048
        AO = XRO + 2072
        xn = area(S[0], 2048).rearrange("p (t n) -> p t n", t=TT)
        xrec = area(XRO, 8 * 259).rearrange("p (k n) -> p k n", k=8)
        xc = area(S[1], 2048).rearrange("p (k n) -> p k n", k=8)
        gate = area(S[2], 2048).rearrange("p (k n) -> p k n", k=8)
        rg = area(S[3], 2048).rearrange("p (k n) -> p k n", k=8)
        ig = area(S[4], 2048).rearrange("p (k n) -> p k n", k=8)
        av = area(AO, 2048).rearrange("p (k n) -> p k n", k=8)
        sq = area(XRO, 2048).rearrange("p (k n) -> p k n", k=8)
        up = area(S[1], 1024).rearrange("p (b m n) -> p b m n", b=2, m=2)
        kT = area(S[1], 2048).rearrange("p (k n) -> p k n", k=8)
        qT = area(S[2], 2048).rearrange("p (k n) -> p k n", k=8)
        vtok = area(S[3], 2048).rearrange("p (t n) -> p t n", t=TT)
        kq = area(S[4], 2048).rearrange("p (t n) -> p t n", t=TT)
        bias1 = area(XRO, 4096).rearrange("p (h n) -> p h n", h=16)
        prob3 = area(S[0], 1152).rearrange("p (b n) -> p b n", b=3)
        probT3 = area(S[0] + 1152, 768).rearrange("p (b n) -> p b n", b=2)
        prob_me = area(S[0], 1024).rearrange("p (b n) -> p b n", b=2)
        probT_me = area(S[0] + 1024, 1024).rearrange("p (b n) -> p b n", b=2)
        qT_mb = area(S[1], 1024).rearrange("p (k n) -> p k n", k=4)
        kT_mb = area(S[1] + 1024, 1024).rearrange("p (k n) -> p k n", k=4)
        qT_sw = area(S[2], 1024).rearrange("p (k n) -> p k n", k=4)
        qT_me = area(S[2] + 1024, 1024).rearrange("p (k n) -> p k n", k=4)
        v_mb = area(S[3], 1024).rearrange("p (t n) -> p t n", t=TT)
        kT_sw = area(S[3] + 1024, T)
        v_sw = area(S[3] + 1536, 256).rearrange("p (t n) -> p t n", t=TT)
        gA, gB = (area(o, 2048).rearrange("p (k n) -> p k n", k=8) for o in (S[4], XRO))
        g_br = [gA, gB, gA]
        merged = kT
        fu = area(S[1], 4 * 258).rearrange("p (k n) -> p k n", k=4)
        fc = area(S[2], 4 * 256).rearrange("p (k n) -> p k n", k=4)
        gpost = area(S[3], 2048).rearrange("p (t n) -> p t n", t=2)
        rows_in = area(S[1], 512).rearrange("p (k n) -> p k n", k=4)
        erow = area(S[2], 768).rearrange("p (k n) -> p k n", k=2)
        onehot = area(S[3], 384)
        relb = area(S[3] + 512, 16)

        s_landed = [sem(f"landed{i}") for i in range(SLOTS)]
        s_hi = sem("split_hi")
        s_lo = sem("split_lo")
        s_step = sem("pe_steps")
        s_evac = sem("group_evac")
        s_bev = sem("token_evac")
        s_tok = sem("piece_done")
        s_add = sem("piece_added")
        s_ss, s_rstd = sem("sumsq"), sem("rstd_ready")
        s_ms, s_rms = sem("meansq_kq"), sem("rootmeansq_kq")
        s_xn, s_xnT = sem("xn_ready"), sem("xn_transposed")
        s_xhi, s_xlo = sem("x_hi"), sem("x_lo")
        s_chain = sem("dve_chain")
        s_achain = sem("act_chain")
        s_pchain = sem("pool_chain")
        s_const = sem("constants")
        s_ident = sem("identity")
        s_small, s_small2, s_tables = sem("small_loads"), sem("small_loads_pool"), sem("bias_table_loads")
        s_x = sem("x_loaded")
        s_mem = sem("mem_loaded")
        s_vT, s_vec = sem("vectors_transposed"), sem("vectors_ready")
        s_e1, s_eps, s_e2 = sem("rel_rows"), sem("rel_psum"), sem("rel_rows2")
        s_ew = sem("bias_rows_written")
        s_b1l, s_b1 = sem("bias1_loaded"), sem("bias1_masked")
        s_b2l, s_b2 = sem("bias2_loaded"), sem("bias2_masked")
        s_sp0, s_sp1, s_spz, s_cc = sem("softplus_in"), sem("softplus_in2"), sem("softplus_exp"), sem("decay_scale")
        s_convd, s_ch, s_cl = sem("conv_done"), sem("conv_hi"), sem("conv_lo")
        s_lru = sem("lru_gates")
        s_ix = sem("gated_input")
        s_a, s_q, s_sq, s_y, s_yh, s_yl = (
            sem("decay"), sem("input_scale2"), sem("input_scale"),
            sem("rec_out"), sem("rec_out_hi"), sem("rec_out_lo"))
        s_relu, s_hh, s_hl = sem("relu"), sem("hidden_hi"), sem("hidden_lo")
        s_kq2, s_kqn, s_kqT, s_kqev = (
            sem("kq_squares"), sem("kq_normed"), sem("kq_transposed"), sem("kq_evac"))
        s_S, s_Sfree, s_max, s_exp, s_p, s_pt, s_ptc, s_pv = (
            sem("scores"), sem("scores_read"), sem("row_max"), sem("exps"), sem("probs"),
            sem("probs_transposed"), sem("probsT"), sem("pv"))
        s_ohi, s_olo = sem("attn_hi"), sem("attn_lo")
        s_sum, s_mh, s_ml = sem("branch_added"), sem("merged_hi"), sem("merged_lo")
        s_conv2, s_gelu2, s_prod, s_fh, s_fl = (
            sem("ffn_conv"), sem("ffn_gelu"), sem("ffn_prod"), sem("ffn_hi"), sem("ffn_lo"))
        s_gp = sem("post_gains")
        s_out = sem("out_written")

        block = ctx.enter_context(nc.Block())

        W8 = lambda w, s: w[:, s, :].rearrange("p (k n) -> p k n", k=KT)
        W2 = lambda w, s: w[:, s, :].rearrange("p (k n) -> p k n", k=2)
        W4 = lambda w, s: w[:, s, :].rearrange("p (k n) -> p k n", k=4)

        def swq(w, s, j):
            v = w[:, s, :]
            return (v.rearrange("p (k j h n) -> p k j h n", k=KT, j=2, h=2)[:, :, j],
                    v.rearrange("p (k h j n) -> p k h j n", k=KT, h=2, j=2)[:, :, :, j])

        def mlp_base(layer):
            return (U_MLP0, G_MLP0, 0) if layer == 0 else (U_MLP1, G_MLP1, 16)

        def out_of(H):
            return H // 2 if H < 32 else 16 + (H - 32)

        def ends_out(H):
            return H >= 32 or H % 2 == 1

        def attn_dst(o):
            return (XB, o) if o < 8 else (XB, (o - 8) % 8)

        BY_POOL, BY_SP, BY_ACT = 5, 7, 6
        ubr = area(S[2], 1024).rearrange("p (b n) -> p b n", b=4)

        def xnT(bank, k):
            b = bank + 2 * (k // 4)
            return PS[:, b:b + 2, P * (k % 4):P * (k % 4) + P]

        def place_of(H):
            if H < 32:
                return prob3[:, H % 3, :], probT3[:, H % 2, :], H % 3
            return prob_me[:, H % 2, :], probT_me[:, H % 2, :], H % 3

        def score_bank(H):
            return 2 + H % 2

        def pt_bank(H):
            return 0 if H < 16 else 4 + H % 2

        def out_bank(H):
            return 1 if H < 16 else 6 + out_of(H) % 2

        SPLIT_AT = {5: U_O, 9: U_O + 1, 13: U_O + 2}
        POOL_SPLIT_MEM = [u + LEAD for u in range(U_MEMK, U_MEMV + 2)]
        POOL_SPLIT_O = [u + LEAD for u in (U_V + 3, U_O, U_O + 1, U_O + 2)]

        def pieces(bank0=4):
            return [(t, c, bank0 + 2 * t + c) for t in range(TT) for c in range(2)]

        NORM_HI = [8 * n + (8 if n > 3 else 0) for n in range(8)]

        small_loads = []

        def small(dst, src):
            small_loads.append(lambda queue, done=s_small: queue.dma_start(dst, src).then_inc(done, 16))

        def vec(name, row, n):
            src = A[name].rearrange("a n -> (a n)") if len(A[name].shape) == 2 else A[name]
            small(rows_in[row:row + n, 0, :], src.rearrange("(k n) -> k n", n=P))

        vec("a_norm", R_ANORM, 8)
        vec("kv_norm", R_KV, 8)
        vec("b_norm", R_B, 8)
        vec("mlp_norm", R_MLP, 16)
        vec("norm_mix_pre_2", R_MIX, 8)
        vec("norm_ffn_pre_2", R_FFN, 8)
        vec("norm_mem_2", R_MEM, 8)
        vec("a_conv_b", R_CB, 8)
        small(rows_in[R_CW:R_CW + 32, 0, :], A["a_conv_w"][0].rearrange("w (k n) -> (w k) n", n=P))
        vec("a_lambda", R_LAM, 8)
        small(rows_in[R_BG:R_BG + 16, 0, :], A["a_b_gate"][0].rearrange("b (k n) -> (b k) n", n=P))
        fw = A["ffn_conv_w_2"][0].rearrange("w (k n) -> (w k) n", n=P)
        small(rows_in[0:88, 1, :], fw[0:88])
        small(rows_in[0:44, 2, :], fw[88:132])
        small(rows_in[44:88, 2, :], A["ffn_conv_b_2"][0].rearrange("(k n) -> k n", n=P))
        for r, name in enumerate(("k_norm", "b_q_norm")):
            src = A[name] if r == 0 else A[name][0]
            for half_ in range(2):
                small(rows_in[r:r + 1, 3, 64 * half_:64 * half_ + 64], src.rearrange("(a n) -> a n", a=1))

        @block.sync
        def _(sp):
            sp.dma_start(res[:], A["x"][0].rearrange("(t p) n -> p t n", p=P)).then_inc(s_x, 16)

            def load(u, slot, value):
                if value is not None:
                    sp.wait_ge(s_lo, value)
                dst = raw[:, slot, :].rearrange("p (k n) -> p k n", k=w_units[u].shape[1])
                if u in U_SWQ:
                    for h in range(2):
                        sp.dma_start(dst[:, :, P * h:P * h + P], w_units[u][:, :, h, :]).then_inc(s_landed[slot], 16)
                    return
                sp.dma_start(dst, w_units[u]).then_inc(s_landed[slot], 16)

            for u in range(N_UNITS):
                load(u, u % SLOTS, u - SLOTS + 1 if u >= SLOTS else None)
                if u == 0:
                    for load_small in small_loads[BY_POOL:BY_POOL + BY_SP]:
                        load_small(sp)
                if u == 3:
                    sp.wait_ge(s_xnT, 1)
                    sp.dma_start(xn, A["mem_2"][0].rearrange("(t p) n -> p t n", p=P)).then_inc(s_mem, 16)
            for t in range(TT):
                sp.wait_ge(s_add, 4 * A_FFN + 2 * t + 2)
                sp.dma_start(out[0, P * t:P * t + P, :], res[:, t, :]).then_inc(s_out, 16)
            sp.wait_ge(s_out, 16 * TT)

        @block.gpsimd
        def _(pool):
            pool.memset(ident[:], 0.0).then_inc(s_ident, 1)
            pool.wait_ge(s_ident, 1)
            pool.affine_select(out=ident[:], in_=ident[:], compare_op=ALU.not_equal, fill=1.0, base=0,
                               pattern=[[-1, P]], channel_multiplier=1).then_inc(s_ident, 1)
            pool.memset(mhalf[:], -0.5).then_inc(s_const, 1)
            for load_small in small_loads[:BY_POOL]:
                load_small(pool, s_small2)

            pool.wait_ge(s_const, 1)
            chain = [0]

            def link(ins):
                chain[0] += 1
                ins.then_inc(s_pchain, 1)
                pool.wait_ge(s_pchain, chain[0])

            def roots(b):
                for t in range(TT):
                    pool.wait_ge(s_ss, 4 * b + 2 * t + 2)
                    link(pool.tensor_scalar(ss[:, 4 + t:5 + t], ss[:, 2 * t:2 * t + 1], ss[:, 2 * t + 1:2 * t + 2], EPS,
                                            ALU.add, ALU.add))
                    pool.tensor_tensor(rstd[:, t:t + 1], ss[:, 4 + t:5 + t], mhalf[:, 0:1], ALU.pow).then_inc(s_rstd, 1)

            def split(u):
                pool.wait_ge(s_lo, u)
                pool.wait_ge(s_hi, u + 1)
                pool.tensor_tensor(wlo[:, u % SLOTS, :], raw[:, u % SLOTS, :], whi[:, u % SLOTS, :].bitcast(F32),
                                   ALU.subtract).then_inc(s_lo, 1)

            def toeplitz(dst, row0, heads):
                src = bass.AP(bias_rows.tensor, row0 * 384 + 1, [[1, P], [384, heads], [1, T]])
                return pool.dma_start(dst, src)

            roots(SQ_NORM[0])
            TABLES = ((erow[0:16, 0, 65:65 + NREL], A["b_rel_bias"][0]), (relb[0:32, :], A["rel_bias_2"]),
                      (onehot[0:32, :], A["bucket_onehot"]), (sinks[:], A["swa_sinks_2"][0].partition_broadcast(P)))
            for dst, src in TABLES:
                pool.dma_start(dst, src).then_inc(s_tables, 16)
            pool.wait_ge(s_sp1, 1)
            link(pool.tensor_tensor(sp_a[:], sp_b[:], sp_b[:], ALU.mult))
            TERMS = 9
            link(pool.tensor_scalar(cneg[:], sp_a[:], 2.0 / (2 * TERMS + 1), 2.0 / (2 * TERMS - 1), ALU.mult, ALU.add))
            for n in range(TERMS - 2, -1, -1):
                link(pool.tensor_tensor(cneg[:], cneg[:], sp_a[:], ALU.mult))
                link(pool.tensor_scalar(cneg[:], cneg[:], 1.0, 2.0 / (2 * n + 1), ALU.mult, ALU.add))
            link(pool.tensor_tensor(cneg[:], cneg[:], sp_b[:], ALU.mult))
            link(pool.tensor_tensor(cneg[:], cneg[:], sp_c[:], ALU.add))
            link(pool.tensor_scalar(cpos[:], cneg[:], LRU_C, 0.0, ALU.mult, ALU.add))
            pool.tensor_scalar(cneg[:], cneg[:], -LRU_C, 0.0, ALU.mult, ALU.add).then_inc(s_cc, 1)
            pool.wait_ge(s_e1, 2)
            pool.dma_start(bias_rows[0:16, :], erow[0:16, 0, :]).then_inc(s_ew, 16)
            pool.wait_ge(s_e2, 1)
            pool.dma_start(bias_rows[16:32, :], erow[0:16, 1, :]).then_inc(s_ew, 16)
            for k in range(KT):
                if k == KT - 2:
                    roots(SQ_NORM[1])
                pool.wait_ge(s_ch, k + 1)
                pool.tensor_tensor(XB[:, k, 1, :], xc[:, k, :], XB[:, k, 0, :].bitcast(F32), ALU.subtract)\
                    .then_inc(s_cl, 1)
            for h in range(2):
                pool.wait_ge(s_lru, 4 * h + 4)
                v = ig[:, 4 * h:4 * h + 4, :]
                pool.tensor_tensor(v, v, xc[:, 4 * h:4 * h + 4, :], ALU.mult).then_inc(s_ix, 1)
            for u in POOL_SPLIT_MEM:
                split(u)
            pool.wait_ge(s_ew, 32)
            roots(SQ_NORM[2])
            toeplitz(bias1, 0, 16).then_inc(s_b1l, 16)
            pool.wait_ge(s_b1l, 16)
            pool.memset(bias1[0:CHUNK, :, 0:CHUNK], MASKED).then_inc(s_b1, 1)
            roots(SQ_NORM[3])
            for u in POOL_SPLIT_O:
                split(u)
            pool.wait_ge(s_Sfree, 16)
            toeplitz(bias1, 16, 16).then_inc(s_b2l, 16)
            roots(SQ_NORM[4])
            pool.wait_ge(s_b2l, 16)
            pool.affine_select(out=bias1[:, :, 0:P], in_=bias1[:, :, 0:P], compare_op=ALU.is_ge, fill=MASKED,
                               base=1 - P, pattern=[[0, 16], [1, P]], channel_multiplier=1).then_inc(s_b2, 1)
            pool.affine_select(out=bias1[:, 8:16, P:T], in_=bias1[:, 8:16, P:T], compare_op=ALU.is_ge, fill=MASKED,
                               base=P - 2, pattern=[[0, 8], [-1, P]], channel_multiplier=-1).then_inc(s_b2, 1)
            roots(SQ_NORM[5])
            for b in (1, 2):
                if b == 2:
                    pool.wait_ge(s_pv, 36)
                    for i, name in enumerate(("norm_mix_post_2", "norm_ffn_post_2")):
                        pool.dma_start(gpost[:, i, :], A[name][0].partition_broadcast(P)).then_inc(s_gp, 16)
                for k in range(8):
                    g = G_BR[b] + k
                    pool.wait_ge(s_evac, g + 1)
                    pool.tensor_tensor(merged[:, k, :], merged[:, k, :], ubr[:, g % 4, :], ALU.add).then_inc(s_sum, 1)
            roots(SQ_POST[0])
            roots(SQ_NORM[6])
            roots(SQ_POST[1])

        @block.scalar
        def _(act):
            chain = [0]

            def link(ins):
                chain[0] += 1
                ins.then_inc(s_achain, 1)
                act.wait_ge(s_achain, chain[0])

            def split(u, it=0, units=0, steps=0, part=None):
                if u is None or u >= N_UNITS:
                    return
                s = u % SLOTS
                act.wait_ge(s_landed[s], it * (16 * units // SLOTS) + LANDED(u))
                if u >= SLOTS:
                    act.wait_ge(s_step, it * steps + AFTER[u - SLOTS])
                if u in U_SWQ:
                    act.activation(swq(whi, s, 0)[0], swq(raw, s, 0)[1], ACT.Copy)
                    act.activation(swq(whi, s, 1)[0], swq(raw, s, 1)[1], ACT.Copy).then_inc(s_hi, 1)
                    return
                if part is not None:
                    c = UNIT // 2 * part
                    ins = act.activation(whi[:, s, c:c + UNIT // 2], raw[:, s, c:c + UNIT // 2], ACT.Copy)
                    if part == 1:
                        ins.then_inc(s_hi, 1)
                    return
                act.activation(whi[:, s, :], raw[:, s, :], ACT.Copy).then_inc(s_hi, 1)

            def evac(g, step, dst, func=ACT.Copy, scale=1.0):
                act.wait_ge(s_step, step)
                act.activation(dst, PS[:, bank_of(g), 0:T], func, scale=scale).then_inc(s_evac, 1)

            def unit_a(u, g, dsts, func=ACT.Copy, scale=1.0):
                split(u + LEAD)
                for m, dst in enumerate(dsts):
                    evac(g + m, BEFORE(u) + m + 1, dst, func, scale)

            def unit_b(u):
                split(u + LEAD)

            def squares(b, src, ready):
                for i, (t, c, bank) in enumerate(pieces()):
                    ready(i)
                    v = PS[:, bank, :] if src is None else src[:, t, 512 * c:512 * c + 512]
                    junk = xn[:, t, 512 * c:512 * c + 512] if src is None else PS[:, bank, :]
                    if b == SQ_NORM[1]:
                        junk = av[:, 2 * i:2 * i + 2, :].rearrange("p a b -> p (a b)")
                    act.activation(junk, v, ACT.Square, scale=D ** -0.5, accum_out=ss[:, i:i + 1]).then_inc(s_ss, 1)

            def added(product):
                return lambda i: act.wait_ge(s_add, 4 * product + i + 1)

            def norm(n, src, outs, ready, bank=0):
                squares(SQ_NORM[n], src, ready)
                norm_hi(n, outs, bank)

            def norm_hi(n, outs, bank=0):
                act.wait_ge(s_xnT, n + 1)
                if n == 0:
                    act.wait_ge(s_vec, 1)
                i = 0
                for X, row in outs:
                    for k in KO:
                        if i >= 2:
                            act.wait_ge(s_xlo, NORM_HI[n] + i - 1)
                        act.activation(X[:, k, 0, :].rearrange("p (t n) -> p t n", t=TT), xnT(bank, k), ACT.Copy,
                                       scale=vecs[:, row + k:row + k + 1]).then_inc(s_xhi, 1)
                        i += 1

            for load_small in small_loads[BY_POOL + BY_SP:]:
                load_small(act)

            squares(SQ_NORM[0], res, lambda i: act.wait_ge(s_x, 16))
            split(0)
            norm_hi(0, [(XA, R_ANORM)])
            split(1)
            split(2)
            act.wait_ge(s_sp0, 1)
            act.activation(sp_b[:], sp_a[:], ACT.Exp, scale=-1.0).then_inc(s_spz, 1)

            def rec_unit(i):
                u, g = U_REC[i], G_REC[i]
                split(u + LEAD)
                for m, k in enumerate((2 * i, 2 * i + 1)):
                    act.wait_ge(s_step, BEFORE(u) + m + 1)
                    v = PS[:, bank_of(g + m), 0:T]
                    act.activation(xrec[:, k, 3:3 + T], v, ACT.Copy)
                    act.activation(xc[:, k, :], v, ACT.Identity, scale=vecs[:, R_CW + 24 + k:R_CW + 25 + k],
                                   bias=vecs[:, R_CB + k:R_CB + k + 1]).then_inc(s_evac, 1)

            def conv_hi(i):
                for k in (2 * i, 2 * i + 1):
                    act.wait_ge(s_convd, k + 1)
                    act.activation(XB[:, k, 0, :], xc[:, k, :], ACT.Copy).then_inc(s_ch, 1)

            def gate_unit(i):
                unit_a(U_GATE[i], G_GATE[i], [gate[:, 2 * i + m, :] for m in range(2)], ACT.Gelu_apprx_tanh)

            rec_unit(0)
            rec_unit(1)
            conv_hi(0)
            act.wait_ge(s_ew, 32)
            gate_unit(0)
            conv_hi(1)
            rec_unit(2)
            gate_unit(1)
            conv_hi(2)
            squares(SQ_NORM[1], xn, lambda i: act.wait_ge(s_mem, 16))
            rec_unit(3)
            gate_unit(2)
            conv_hi(3)
            gate_unit(3)
            for n in range(8):
                act.wait_ge(s_step, BEFORE(U_LRU) + n + 1)
                for e, dst in enumerate((rg, ig)):
                    ins = act.activation(dst[:, n, :], PS[:, 4 + n % 4, T * e:T * e + T], ACT.Sigmoid,
                                         bias=vecs[:, R_BG + 2 * n + e:R_BG + 2 * n + e + 1])
                ins.then_inc(s_lru, 1)
            split(U_LRU + LEAD)
            norm_hi(1, [(XB, R_MEM)], bank=4)
            split(U_MEMK + LEAD)
            act.wait_ge(s_lru, 8)
            act.wait_ge(s_cc, 1)
            for h in range(2):
                for n in range(4 * h, 4 * h + 4):
                    act.activation(av[:, n, :], rg[:, n, :], ACT.Exp, scale=cneg[:, n:n + 1]).then_inc(s_a, 1)
                for n in range(4 * h, 4 * h + 4):
                    act.activation(rg[:, n, :], rg[:, n, :], ACT.Tanh, scale=cpos[:, n:n + 1]).then_inc(s_a, 1)
                for m in range(2):
                    evac(G_MEMK + 2 * h + m, BEFORE(U_MEMK + h) + m + 1, kT_me[:, 2 * h + m, :])
            for h in range(2):
                act.wait_ge(s_q, h + 1)
                act.activation(rg[:, 4 * h:4 * h + 4, :], rg[:, 4 * h:4 * h + 4, :], ACT.Sqrt).then_inc(s_sq, 1)
            split(U_MEMK + 1 + LEAD)
            split(U_MEMV + LEAD)
            for k in range(2):
                act.wait_ge(s_y, k + 1)
                act.activation(XA[:, 4 * k:4 * k + 4, 0, :], xc[:, 4 * k:4 * k + 4, :], ACT.Copy).then_inc(s_yh, 1)
            unit_b(U_MEMV + 1)
            for i in range(4):
                unit_b(U_ROUT + i)

            def mlp(layer):
                u0, g0, _ = mlp_base(layer)
                st0 = BEFORE(u0)

                def hid(j, it=0):
                    act.wait_ge(s_evac, it * 4 + g0 + 2 * j + 2)
                    act.activation(XB[:, 2 * (j % 2):2 * (j % 2) + 2, 0, :], up[:, j % 2], ACT.Copy).then_inc(s_hh, 1)

                def relu(g, dst, step, it=0):
                    act.wait_ge(s_step, it * 6 + step)
                    act.activation(dst, PS[:, bank_of(g), 0:T], ACT.Relu).then_inc(s_relu, 1)

                split(u0 + LEAD)
                for m in range(2):
                    relu(g0 + m, up[:, 0, m, :], st0 + m + 1)
                hid(0)

                def pair_(i, it=0):
                    kw = dict(it=it, units=4, steps=6)
                    split(u0 + 1 + 2 * i + LEAD, **kw)
                    for m in range(2):
                        relu(g0 + 2 * i + 2 + m, up[:, (i + 1) % 2, m, :], st0 + 2 + 3 * i + m + 1, it)
                    split(u0 + 2 + 2 * i + LEAD, **kw)
                    hid(i + 1, it)

                with act.Fori(0, 7) as it:
                    pair_(0, it)
                    pair_(1, it)
                pair_(14)
                split(u0 + MLP_UNITS - 1 + LEAD)

            norm(2, res, [(XA, R_MLP)], added(A_ROUT))
            mlp(0)

            norm(3, res, [(XA, R_KV), (XB, R_B)], added(A_MLP0))
            for i in range(4):
                unit_b(U_K + i)

            def kq_square(r):
                act.wait_ge(s_bev, (B_K, B_Q)[r] + 1)
                act.activation(xn, kq, ACT.Square, scale=0.125).then_inc(s_kq2, 1)

            def kq_root(r):
                act.wait_ge(s_ms, r + 1)
                act.activation(rstd[:, 0:32], ss[:, 32:64], ACT.Sqrt).then_inc(s_rms, 1)

            def kq_evac(r):
                act.wait_ge(s_kqT, r + 1)
                b0 = 4 if r == 0 else 0
                for b in range(4):
                    act.activation((kT, qT)[r][:, 2 * b:2 * b + 2, :], PS[:, b0 + b, :].rearrange("p (k n) -> p k n", k=2),
                                   ACT.Copy, scale=headg[:, r:r + 1]).then_inc(s_kqev, 1)

            unit_b(U_Q)
            kq_square(0)
            unit_b(U_Q + 1)
            kq_root(0)
            unit_b(U_Q + 2)
            kq_evac(0)
            unit_b(U_Q + 3)
            unit_b(U_V)
            kq_square(1)
            unit_b(U_V + 1)
            kq_root(1)
            unit_b(U_V + 2)
            kq_evac(1)
            unit_b(U_V + 3)

            def values_out():
                act.wait_ge(s_step, AFTER[U_V + 3])
                act.activation(vtok[:, 0, :], PS[:, 4:6, :].rearrange("p a b -> p (a b)"), ACT.Copy).then_inc(s_bev, 1)

            def exps(H):
                pr, _, r = place_of(H)
                act.wait_ge(s_max, H + 1)
                if H < 32:
                    act.activation(pr[:, 0:P], pr[:, 0:P], ACT.Exp, bias=snmax[:, r, 0:1],
                                   accum_out=ssum[:, r, 0:1])
                    ins = act.activation(pr[:, P:3 * P], pr[:, P:3 * P], ACT.Exp, bias=snmax[:, r, 1:2],
                                         accum_out=ssum[:, r, 1:2])
                else:
                    act.wait_ge(s_pt, max(H - 1, 32))
                    for t in range(TT):
                        ins = act.activation(pr[:, T * t:T * t + T], PS[:, score_bank(H), T * t:T * t + T], ACT.Exp,
                                             bias=snmax[:, r, t:t + 1], accum_out=ssum[:, r, t:t + 1])
                if 24 <= H < 32:
                    ins = act.activation(ssink[:, r, :], snmax[:, r, :], ACT.Exp, bias=sinks[:, H - 24:H - 23])
                ins.then_inc(s_exp, 1)

            def probs_out(H):
                n = 384 if H < 32 else 512
                act.wait_ge(s_pt, H + 1)
                if H >= 2:
                    act.wait_ge(s_pv, H - 1 if H < 32 else max(H - 1, 32))
                act.activation(place_of(H)[1][:, 0:n], PS[:, pt_bank(H), 0:n], ACT.Copy).then_inc(s_ptc, 1)

            def attn_hi(H):
                if not ends_out(H):
                    return
                o = out_of(H)
                act.wait_ge(s_pv, H + 1)
                X, k = attn_dst(o)
                if o >= 8:
                    if (o - 8) % 4 == 0 and o >= 16:
                        act.wait_ge(s_step, AFTER[U_BR[0] + 1])
                act.activation(X[:, k, 0, :], PS[:, out_bank(H), 0:T], ACT.Copy).then_inc(s_ohi, 1)

            exps(0)
            exps(1)
            values_out()
            for H in range(16):
                if H < 4:
                    probs_out(H)
                if H + 2 < 16:
                    exps(H + 2)
                if H >= 4:
                    probs_out(H)
                if H:
                    attn_hi(H - 1)
                if H in SPLIT_AT:
                    split(SPLIT_AT[H] + LEAD, part=0)
                if H - 1 in SPLIT_AT:
                    split(SPLIT_AT[H - 1] + LEAD, part=1)
            attn_hi(15)
            unit_b(U_O + 3)

            norm(4, res, [(XA, R_MLP + 8)], added(A_O))
            mlp(1)

            norm(5, res, [(XA, R_MIX)], added(A_MLP1))
            two = lambda v, i: [v[:, 2 * i + m, :] for m in range(2)]
            for i in range(2):
                unit_a(U_QKV + i, G_QMB + 2 * i, two(qT_mb, i), scale=0.125)
            for i in range(2):
                unit_a(U_QKV + 2 + i, G_KMB + 2 * i, two(kT_mb, i))
            for i in range(2):
                unit_b(U_QKV + 4 + i)
            for i in range(2):
                unit_a(U_QKV + 6 + i, G_QSW + 2 * i, two(qT_sw, i), scale=0.125)
            unit_a(U_QKV + 8, G_KSW, [kT_sw])
            for i in range(2):
                unit_a(U_QKV + 9 + i, G_QME + 2 * i, two(qT_me, i), scale=float(P) ** -0.5)

            def gates(b, k, H, last):
                if k % 2 == 0:
                    split(U_G2[b] + k // 2 + LEAD)
                if H < last:
                    exps(H + 1)
                evac(G_G2[b] + k, BEFORE(U_G2[b]) + k + 1, g_br[b][:, k, :], ACT.Tanh, 0.5)
                if H <= last:
                    probs_out(H)
                if H - 1 <= last and k:
                    attn_hi(H - 1)

            exps(16)
            for k in range(8):
                gates(0, k, 16 + k, 31)
            attn_hi(23)
            for k in range(8):
                gates(1, k, 24 + k, 31)
            split(U_BR[0] + LEAD)
            attn_hi(31)
            split(U_BR[0] + 1 + LEAD)
            exps(32)
            act.wait_ge(s_evac, G_G2[2])
            for k in range(8):
                gates(2, k, 32 + k, 35)
            for b in (1, 2):
                for i in range(2):
                    split(U_BR[b] + i + LEAD)
            for k in range(2):
                act.wait_ge(s_sum, 8 + 4 * (k + 1))
                act.activation(XA[:, 4 * k:4 * k + 4, 0, :], merged[:, 4 * k:4 * k + 4, :], ACT.Copy, scale=0.5)\
                    .then_inc(s_mh, 1)
            for i in range(4):
                unit_b(U_OUT2 + i)

            def product(i_product, u_last):
                return lambda i: act.wait_ge(*((s_tok, 3 * i_product + i + 1) if i < 3 else (s_step, AFTER[u_last])))

            squares(SQ_POST[0], None, product(A_OUT2, U_OUT2 + 3))
            norm(6, res, [(XA, R_FFN)], added(A_OUT2))

            def ffn_evac(u, g0, e, j):
                for m in range(2):
                    f, c = 2 * e + m, e * 22 + 2 * j + m
                    act.wait_ge(s_step, BEFORE(u) + m + 1)
                    v = PS[:, bank_of(g0 + m), 0:T]
                    act.activation(fu[:, f, 2:2 + T], v, ACT.Copy)
                    act.activation(fc[:, f, :], v, ACT.Identity, scale=fvec[:, 1, c:c + 1],
                                   bias=fvec[:, 1, 44 + c:45 + c]).then_inc(s_evac, 1)

            for j in range(FFN_STEPS):
                u = U_FFN if j == 0 else U_FFN + 2 + 3 * (j - 1)
                split(u + LEAD)
                if j:
                    act.wait_ge(s_fl, j)
                ffn_evac(u, G_FFN + 4 * j, 0, j)
                split(u + 1 + LEAD)
                act.wait_ge(s_conv2, 2 * j + 1)
                act.activation(fc[:, 0:2, :], fc[:, 0:2, :], ACT.Gelu_apprx_tanh).then_inc(s_gelu2, 1)
                ffn_evac(u + 1, G_FFN + 4 * j + 2, 1, j)
                if j:
                    split(u + 2 + LEAD)
                act.wait_ge(s_prod, j + 1)
                act.activation(XB[:, 2 * (j % 2):2 * (j % 2) + 2, 0, :], fc[:, 0:2, :], ACT.Copy).then_inc(s_fh, 1)
            squares(SQ_POST[1], None, product(A_FFN, N_UNITS - 1))

        @block.tensor
        def _(pe):
            def group(g, slot, m, view, ktiles, X, it=0, groups=0, k0=0, xready=None):
                if g >= ring_of(g):
                    pe.wait_ge(s_evac, it * groups + g - ring_of(g) + 1)
                hi, lo = view(whi, slot), view(wlo, slot)
                for i, k in enumerate(KO if ktiles == KT else range(ktiles)):
                    if xready is not None:
                        pe.wait_ge(s_xlo, xready + i + 1)
                    for w, part in ((hi, 0), (hi, 1), (lo, 0)):
                        ins = pe.matmul(PS[:, bank_of(g), 0:T], w[:, k, P * m:P * m + P], X[:, k0 + k, part, :],
                                        start=(i == 0 and part == 0 and w is hi), stop=(i == ktiles - 1 and w is lo),
                                        skip_group_check=True)
                ins.then_inc(s_step, 1)

            def have(u, it=0, units=0):
                pe.wait_ge(s_lo, it * units + u + 1)

            def unit_a(u, g, X=XA, xready=None):
                have(u)
                for m in range(2):
                    group(g + m, u % SLOTS, m, W8, KT, X, xready=xready if m == 0 else None)

            def tokens(slot, view, ktiles, X, k0, bank, n, first, last, c0=0, width=512, pieces_=False):
                hi, lo = view(whi, slot), view(wlo, slot)

                def add(t, c, k, part, w, opens, closes):
                    return pe.matmul(PS[:, bank + n * t + c, 0:width], X[:, k0 + k, part, P * t:P * t + P],
                                     w[:, k, c0 + 512 * c:c0 + 512 * c + width], start=opens, stop=closes,
                                     skip_group_check=True)

                if last and pieces_:
                    for t in range(TT):
                        for c in range(n):
                            for k in range(ktiles):
                                for part, w in ((0, hi), (0, lo), (1, hi)):
                                    ins = add(t, c, k, part, w, False, part == 1 and k == ktiles - 1)
                            if (t, c) != (TT - 1, n - 1):
                                ins.then_inc(s_tok, 1)
                    ins.then_inc(s_step, 1)
                    return
                for k in range(ktiles):
                    for t in range(TT):
                        for part, w in ((0, hi), (0, lo), (1, hi)):
                            for c in range(n):
                                ins = add(t, c, k, part, w, first and k == 0 and part == 0 and w is hi,
                                          last and k == ktiles - 1 and part == 1)
                ins.then_inc(s_step, 1)

            def layer_b(u, X, bank=4, pieces_=True, ready=None):
                for i in range(4):
                    have(u + i)
                    if ready is not None:
                        ready(i)
                    tokens((u + i) % SLOTS, W2, 2, X, 2 * i, bank, 2, i == 0, i == 3, pieces_=pieces_)

            def norm_T(n, bank=0):
                for t in range(TT):
                    pe.wait_ge(s_xn, 2 * n + t + 1)
                    for k in range(KT):
                        ins = pe.transpose(PS[:, bank + t + 2 * (k // 4), P * (k % 4):P * (k % 4) + P],
                                           xn[:, t, P * k:P * k + P], ident[:])
                ins.then_inc(s_xnT, 1)

            pe.wait_ge(s_ident, 2)
            norm_T(0)
            pe.wait_ge(s_small, 16 * (BY_SP + BY_ACT))
            pe.wait_ge(s_small2, 16 * BY_POOL)
            pe.transpose(PS[:, 6, 0:P], rows_in[:, 0, :], ident[:])
            for r in range(2):
                pe.transpose(PS[:, 6, P + 88 * r:P + 88 * r + 88], rows_in[0:88, 1 + r, :], ident[0:88, 0:88])
            pe.transpose(PS[:, 6, 384:386], rows_in[0:2, 3, :], ident[0:2, 0:2]).then_inc(s_vT, 1)
            unit_a(U_REC[0], G_REC[0], xready=NORM_HI[0])
            pe.wait_ge(s_tables, 16 * 4)
            pe.matmul(PS[0:16, 7, 0:384], relb[0:32, :], onehot[0:32, :], start=True, stop=True).then_inc(s_eps, 1)
            unit_a(U_REC[1], G_REC[1])
            for i in range(2):
                unit_a(U_GATE[i], G_GATE[i])
                unit_a(U_REC[2 + i], G_REC[2 + i])
            unit_a(U_GATE[2], G_GATE[2])
            unit_a(U_GATE[3], G_GATE[3])
            have(U_LRU)
            s = U_LRU % SLOTS
            for n in range(8):
                pe.wait_ge(s_cl, n + 1)
                if n >= 4:
                    pe.wait_ge(s_lru, n - 3)
                for e in range(2):
                    w, wl = W8(whi, s)[:, n, P * e:P * e + P], W8(wlo, s)[:, n, P * e:P * e + P]
                    dst = PS[:, 4 + n % 4, T * e:T * e + T]
                    pe.matmul(dst, w, XB[:, n, 0, :], start=(e == 0), stop=False, skip_group_check=True)
                    pe.matmul(dst, w, XB[:, n, 1, :], start=False, stop=False, skip_group_check=True)
                    ins = pe.matmul(dst, wl, XB[:, n, 0, :], start=False, stop=(e == 1), skip_group_check=True)
                ins.then_inc(s_step, 1)
            pe.wait_ge(s_lru, 8)
            norm_T(1, bank=4)
            for i in range(2):
                unit_a(U_MEMK + i, G_MEMK + 2 * i, X=XB, xready=NORM_HI[1] if i == 0 else None)
            for i in range(2):
                have(U_MEMV + i)
                if i == 0:
                    pe.wait_ge(s_evac, G_MEMK + 2)
                tokens((U_MEMV + i) % SLOTS, W4, 4, XB, 4 * i, 0, 1, i == 0, i == 1)
            layer_b(U_ROUT, XA, ready=lambda i: pe.wait_ge(s_yl, i // 2 + 1))

            def mlp(layer):
                u0, g0, p0 = mlp_base(layer)
                unit_a(u0, g0, xready=NORM_HI[2 if layer == 0 else 4])

                def down(i, j, first=False, last=False, it=0):
                    have(u0 + 2 + 2 * i if not last else u0 + MLP_UNITS - 1, it, 4)
                    pe.wait_ge(s_hl, it * 2 + p0 + j + 1)
                    s = (u0 + 2 + 2 * i if not last else u0 + MLP_UNITS - 1) % SLOTS
                    tokens(s, W2, 2, XB, 2 * (j % 2), 4, 2, first, last, pieces_=True)

                def up_(i, it=0):
                    u = u0 + 1 + 2 * i
                    have(u, it, 4)
                    for m in range(2):
                        group(g0 + 2 * i + 2 + m, u % SLOTS, m, W8, KT, XA, it, 4)

                up_(0)
                down(0, 0, first=True)
                up_(1)
                down(1, 1)
                with pe.Fori(1, 7) as it:
                    up_(0, it)
                    down(0, 0, it=it)
                    up_(1, it)
                    down(1, 1, it=it)
                up_(14)
                down(14, 14)
                down(15, 15, last=True)

            norm_T(2)
            mlp(0)
            norm_T(3)
            layer_b(U_K, XA, pieces_=False, ready=lambda i: pe.wait_ge(s_xlo, NORM_HI[3] + (3, 7, 8, 8)[i]))
            pe.wait_ge(s_xlo, NORM_HI[3] + 16)

            def kq_T(r):
                b0 = 4 if r == 0 else 0
                pe.wait_ge(s_kqn, r + 1)
                for k in range(KT):
                    for t in range(TT):
                        c = T * (k % 2) + P * t
                        ins = pe.transpose(PS[:, b0 + k // 2, c:c + P], kq[:, t, P * k:P * k + P], ident[:])
                ins.then_inc(s_kqT, 1)

            layer_b(U_Q, XB, bank=0, pieces_=False, ready=lambda i: kq_T(0) if i == 3 else None)
            pe.wait_ge(s_kqev, 4)
            for i in range(3):
                have(U_V + i)
                tokens((U_V + i) % SLOTS, W2, 2, XA, 2 * i, 4, 2, i == 0, False)
            kq_T(1)
            have(U_V + 3)

            def score(H):
                bank = score_bank(H)
                if H in (32, 33):
                    pe.wait_ge(s_evac, G_BR[0] + H - 25)
                elif 2 <= H < 34:
                    pe.wait_ge(s_Sfree, H - 1)
                elif H >= 34:
                    pe.wait_ge(s_exp, H - 1)
                if H < 32:
                    h = H if H < 16 else (H - 16) % 8
                    at, n = ((h % 2), h // 2) if H < 24 else (h // 4, h % 4)
                    q = (qT if H < 16 else qT_mb if H < 24 else qT_sw)[64 * at:64 * at + 64, n, :]
                    k = (kT if H < 16 else kT_mb)[64 * at:64 * at + 64, n, :] if H < 24 else kT_sw[64 * at:64 * at + 64, :]
                    pe.matmul(PS[:, bank, 0:P], q[:, 0:P], k[:, 0:P], start=True, stop=False, skip_group_check=True)
                    ins = pe.matmul(PS[:, bank, P:3 * P], q[:, P:T], k[:, :], start=False, stop=True,
                                    skip_group_check=True)
                else:
                    for t in range(TT):
                        ins = pe.matmul(PS[:, bank, T * t:T * t + T], qT_me[:, H - 32, P * t:P * t + P],
                                        kT_me[:, H - 32, :], start=(t == 0), stop=(t == 1), skip_group_check=True)
                ins.then_inc(s_S, 1)

            CAUSAL = [0, P, 2 * P]
            FULL = [0, 2 * P, P, 3 * P]

            def probs_T(H):
                pe.wait_ge(s_p, H + 1)
                if H >= 1:
                    pe.wait_ge(s_ptc, H if H < 16 else H - 1)
                at = CAUSAL if H < 32 else FULL
                for i, c in enumerate(at):
                    ins = pe.transpose(PS[:, pt_bank(H), P * i:P * i + P], place_of(H)[0][:, c:c + P], ident[:])
                ins.then_inc(s_pt, 1)

            def pv(H):
                o = out_of(H)
                pe.wait_ge(s_ptc, H + 1)
                if o >= 1 and (H >= 32 or H % 2 == 0):
                    pe.wait_ge(s_olo, o if o < 8 else o - 1)
                pT = place_of(H)[1]
                if H < 32:
                    h = H if H < 16 else (H - 16) % 8
                    lo = 64 * (h % 2)
                    v = vtok[:, :, 64 * h:64 * h + 64] if H < 16 else v_mb[:, :, 64 * h:64 * h + 64] if H < 24 \
                        else v_sw[:, :, 64 * (h // 4):64 * (h // 4) + 64]
                    pe.matmul(PS[lo:lo + 64, out_bank(H), 0:T], v[:, 0, :], pT[:, 0:T], start=True, stop=False,
                              skip_group_check=True)
                    ins = pe.matmul(PS[lo:lo + 64, out_bank(H), P:T], v[:, 1, :], pT[:, T:T + P], start=False,
                                    stop=True, skip_group_check=True)
                else:
                    for j in range(2):
                        ins = pe.matmul(PS[:, out_bank(H), 0:T], v_me[:, j, P * (H - 32):P * (H - 32) + P],
                                        pT[:, T * j:T * j + T], start=(j == 0), stop=(j == 1),
                                        skip_group_check=True)
                ins.then_inc(s_pv, 1)

            def part(u, i, k, t, X, opens=False):
                hi, lo = W2(whi, u % SLOTS), W2(wlo, u % SLOTS)
                for part_, w in ((0, hi), (0, lo), (1, hi)):
                    for c in range(2):
                        ins = pe.matmul(PS[:, 4 + 2 * t + c, :], X[:, 2 * i + k, part_, P * t:P * t + P],
                                        w[:, k, 512 * c:512 * c + 512], start=opens and part_ == 0 and w is hi,
                                        stop=False, skip_group_check=True)
                return ins

            for k in range(2):
                for t in range(TT):
                    ins = part(U_V + 3, 3, k, t, XA)
                if k == 0:
                    pe.wait_ge(s_kqev, 8)
                    score(0)
                    score(1)
            ins.then_inc(s_step, 1)
            for H in range(16):
                if H + 2 < 16:
                    score(H + 2)
                if H >= 4:
                    i, k, t = (H - 4) // 4, (H - 4) // 2 % 2, H % 2
                    if t == 0:
                        have(U_O + i)
                        pe.wait_ge(s_olo, 2 * i + k + 1)
                    ins = part(U_O + i, i, k, t, XB, opens=i == 0 and k == 0)
                    if k and t:
                        ins.then_inc(s_step, 1)
                probs_T(H)
                if H == 1:
                    pe.wait_ge(s_bev, B_V + 1)
                if H:
                    pv(H - 1)
            pv(15)
            have(U_O + 3)
            pe.wait_ge(s_olo, 8)
            tokens((U_O + 3) % SLOTS, W2, 2, XB, 6, 4, 2, False, True, pieces_=True)
            norm_T(4)
            mlp(1)
            norm_T(5)
            for i in range(2):
                unit_a(U_QKV + i, G_QMB + 2 * i, xready=NORM_HI[5] if i == 0 else None)
            for i in range(2):
                unit_a(U_QKV + 2 + i, G_KMB + 2 * i)
            for i in range(2):
                have(U_QKV + 4 + i)
                tokens((U_QKV + 4 + i) % SLOTS, W4, 4, XA, 4 * i, 6, 1, i == 0, i == 1)
            for i in range(2):
                unit_a(U_QKV + 6 + i, G_QSW + 2 * i)
            u = U_QKV + 8
            have(u)
            group(G_KSW, u % SLOTS, 0, W8, KT, XA)
            hi, lo = W8(whi, u % SLOTS), W8(wlo, u % SLOTS)
            for t in range(TT):
                for k in range(KT):
                    for part, w in ((0, hi), (0, lo), (1, hi)):
                        ins = pe.matmul(PS[:, 5, P * t:P * t + P], XA[:, k, part, P * t:P * t + P], w[:, k, P:T],
                                        start=(t == 0 and k == 0 and part == 0 and w is hi),
                                        stop=(t == 1 and k == KT - 1 and part == 1), skip_group_check=True)
            ins.then_inc(s_step, 1)
            for i in range(2):
                unit_a(U_QKV + 9 + i, G_QME + 2 * i)
            pe.wait_ge(s_evac, G_QME + 4)
            pe.wait_ge(s_bev, B_VSW + 1)
            def gates(b, k, H, last):
                if H < last:
                    score(H + 1)
                u = U_G2[b] + k // 2
                have(u)
                group(G_G2[b] + k, u % SLOTS, k % 2, W8, KT, XA)
                if H <= last:
                    probs_T(H)
                if H - 1 <= last and k:
                    pv(H - 1)

            def branch(b, k):
                u = U_BR[b] + k // 4
                have(u)
                if k == 2 and b < 2:
                    pe.wait_ge(*((s_Sfree, 32) if b == 0 else (s_exp, 36)))
                group(G_BR[b] + k, u % SLOTS, k % 4, W4, 4, XB, k0=4 * (b % 2))

            score(16)
            for k in range(8):
                gates(0, k, 16 + k, 31)
            pv(23)
            for k in range(8):
                gates(1, k, 24 + k, 31)
            pe.wait_ge(s_olo, 12)
            branch(0, 0)
            pv(31)
            for k in range(1, 8):
                branch(0, k)
            score(32)
            for k in range(8):
                gates(2, k, 32 + k, 35)
            pe.wait_ge(s_olo, 20)
            for b in (1, 2):
                for k in range(8):
                    branch(b, k)
            layer_b(U_OUT2, XA, ready=lambda i: pe.wait_ge(s_ml, i // 2 + 1))
            norm_T(6)

            def up2_(j):
                u = U_FFN if j == 0 else U_FFN + 2 + 3 * (j - 1)
                unit_a(u, G_FFN + 4 * j, xready=NORM_HI[6] if j == 0 else None)
                unit_a(u + 1, G_FFN + 4 * j + 2)

            def down2(j):
                u = U_FFN + 4 + 3 * j if j < FFN_STEPS - 1 else N_UNITS - 1
                have(u)
                pe.wait_ge(s_fl, j + 1)
                tokens(u % SLOTS, W2, 2, XB, 2 * (j % 2), 4, 2, j == 0, j == FFN_STEPS - 1, pieces_=True)

            up2_(0)
            for j in range(FFN_STEPS - 1):
                up2_(j + 1)
                down2(j)
            down2(FFN_STEPS - 1)

        @block.vector
        def _(dve):
            chain = [0]

            def link(ins):
                chain[0] += 1
                ins.then_inc(s_chain, 1)
                dve.wait_ge(s_chain, chain[0])

            def split(u, it=0, units=0):
                if u is None or u >= N_UNITS:
                    return
                s = u % SLOTS
                dve.wait_ge(s_hi, it * units + u + 1)
                if u - 1 in POOL_SPLIT_MEM + POOL_SPLIT_O:
                    dve.wait_ge(s_lo, u)
                if u in U_SWQ:
                    for j in range(2):
                        ins = dve.tensor_tensor(swq(wlo, s, j)[0], swq(raw, s, j)[1], swq(whi, s, j)[0].bitcast(F32),
                                                ALU.subtract)
                    ins.then_inc(s_lo, 1)
                    return
                dve.tensor_tensor(wlo[:, s, :], raw[:, s, :], whi[:, s, :].bitcast(F32), ALU.subtract).then_inc(s_lo, 1)

            def norm(n, src, outs, late=None, bank=0):
                for t in range(TT):
                    dve.wait_ge(s_rstd, ROOTS[SQ_NORM[n]] + t + 1)
                    dve.tensor_scalar(xn[:, t, :], src[:, t, :], rstd[:, t:t + 1], None, ALU.mult).then_inc(s_xn, 1)
                if outs:
                    norm_lo(n, outs, bank, late)

            def norm_lo(n, outs, bank=0, late=None):
                i = NORM_HI[n]
                for o, (X, row) in enumerate(outs):
                    if o == 1:
                        split(late)
                    for k in KO:
                        i += 1
                        dve.wait_ge(s_xhi, i)
                        hi, lo = (X[:, k, j, :].rearrange("p (t n) -> p t n", t=TT) for j in range(2))
                        dve.scalar_tensor_tensor(lo, xnT(bank, k), vecs[:, row + k:row + k + 1], hi.bitcast(F32),
                                                 ALU.mult, ALU.subtract).then_inc(s_xlo, 1)
                if late is not None and len(outs) == 1:
                    split(late)

            def add_out(product, u_last):
                for i, (t, c, bank) in enumerate(pieces()):
                    dve.wait_ge(*((s_tok, 3 * product + i + 1) if i < 3 else (s_step, AFTER[u_last])))
                    v = res[:, t, 512 * c:512 * c + 512]
                    dve.tensor_tensor(v, v, PS[:, bank, :], ALU.add).then_inc(s_add, 1)

            dve.memset(xrec[:, :, 0:3], 0.0)
            norm(0, res, [])
            split(0)
            dve.wait_ge(s_vT, 1)
            link(dve.tensor_copy(vecs[:], PS[:, 6, 0:P]))
            dve.tensor_copy(fvec[:, :, :], PS[:, 6, P:P + 176].rearrange("p (a b) -> p a b", a=2))
            dve.tensor_copy(headg[:, 0:1], PS[:, 6, 384:385])
            dve.tensor_scalar(headg[:, 1:2], PS[:, 6, 385:386], 0.125, None, ALU.mult).then_inc(s_vec, 1)
            norm_lo(0, [(XA, R_ANORM)])
            lam = vecs[:, R_LAM:R_LAM + 8]
            link(dve.tensor_scalar(sp_c[:], lam, -1.0, None, ALU.mult))
            dve.tensor_tensor(sp_a[:], lam, sp_c[:], ALU.max).then_inc(s_sp0, 1)
            link(dve.tensor_scalar(sp_c[:], sp_c[:], 0.0, None, ALU.max))
            split(1)
            split(2)
            dve.wait_ge(s_spz, 1)
            link(dve.tensor_scalar(sp_a[:], sp_b[:], 2.0, None, ALU.add))
            link(dve.reciprocal(sp_a[:], sp_a[:]))
            dve.tensor_tensor(sp_b[:], sp_b[:], sp_a[:], ALU.mult).then_inc(s_sp1, 1)
            dve.wait_ge(s_tables, 16 * 4)
            dve.tensor_copy(erow[0:16, 0, 0:65], erow[0:16, 0, 65:66].to_broadcast([16, 65])).then_inc(s_e1, 1)
            dve.tensor_copy(erow[0:16, 0, 65 + NREL:384],
                            erow[0:16, 0, 64 + NREL:65 + NREL].to_broadcast([16, 384 - 65 - NREL])).then_inc(s_e1, 1)
            dve.wait_ge(s_eps, 1)
            dve.tensor_copy(erow[0:16, 1, :], PS[0:16, 7, 0:384]).then_inc(s_e2, 1)

            def conv(i):
                dve.wait_ge(s_evac, G_REC[i] + 2)
                for w in range(3):
                    for k in (2 * i, 2 * i + 1):
                        ins = dve.scalar_tensor_tensor(xc[:, k, :], xrec[:, k, w:w + T],
                                                       vecs[:, R_CW + 8 * w + k:R_CW + 8 * w + k + 1], xc[:, k, :],
                                                       ALU.mult, ALU.add)
                        if w == 2:
                            ins.then_inc(s_convd, 1)
                    if w < 2:
                        link(ins)

            split(U_REC[0] + LEAD)
            conv(0)
            split(U_REC[1] + LEAD)
            conv(1)
            for i in range(2):
                split(U_GATE[i] + LEAD)
                split(U_REC[2 + i] + LEAD)
                conv(2 + i)
            norm(1, xn, [])
            split(U_GATE[2] + LEAD)
            split(U_GATE[3] + LEAD)

            def half(v, h):
                return v[:, 4 * h:4 * h + 4, :].rearrange("p a b -> p (a b)")

            norm_lo(1, [(XB, R_MEM)], bank=4, late=U_LRU + LEAD)
            for h in range(2):
                dve.wait_ge(s_a, 8 * h + 4)
                link(dve.tensor_tensor(half(sq, h), half(av, h), half(av, h), ALU.mult))
                dve.wait_ge(s_a, 8 * h + 8)
                dve.scalar_tensor_tensor(half(rg, h), half(sq, h), 1.0, half(rg, h), ALU.add, ALU.mult).then_inc(s_q, 1)

            def y_lo(k):
                dve.wait_ge(s_yh, k + 1)
                dve.tensor_tensor(XA[:, 4 * k:4 * k + 4, 1, :], xc[:, 4 * k:4 * k + 4, :],
                                  XA[:, 4 * k:4 * k + 4, 0, :].bitcast(F32), ALU.subtract).then_inc(s_yl, 1)

            dve.wait_ge(s_evac, G_GATE[3] + 2)
            for h in range(2):
                dve.wait_ge(s_sq, h + 1)
                dve.wait_ge(s_ix, h + 1)
                link(dve.tensor_tensor(half(ig, h), half(ig, h), half(rg, h), ALU.mult))
                if h == 1:
                    y_lo(0)
                for k in range(4 * h, 4 * h + 4):
                    ins = dve.tensor_tensor_scan(rg[:, k, :], av[:, k, :], ig[:, k, :], 0.0, ALU.mult, ALU.add)
                link(ins)
                dve.tensor_tensor(half(xc, h), half(rg, h), half(gate, h), ALU.mult).then_inc(s_y, 1)
            y_lo(1)
            dve.wait_ge(s_step, AFTER[U_MEMV + 1])
            dve.tensor_copy(v_me[:], PS[:, 0:2, :]).then_inc(s_bev, 1)
            for i in range(3):
                split(U_ROUT + i + LEAD)
            add_out(A_ROUT, U_ROUT + 3)

            def mlp(layer):
                u0, g0, p0 = mlp_base(layer)


                def relu2(g, dst, it=0):
                    dve.wait_ge(s_relu, it * 4 + 2 * p0 + g - g0 + 1)
                    dve.scalar_tensor_tensor(dst, PS[:, bank_of(g), 0:T], 0.0, dst, ALU.max, ALU.mult).then_inc(s_evac, 1)

                def hid_lo(j, it=0):
                    dve.wait_ge(s_hh, it * 2 + p0 + j + 1)
                    k = 2 * (j % 2)
                    dve.tensor_tensor(XB[:, k:k + 2, 1, :], up[:, j % 2], XB[:, k:k + 2, 0, :].bitcast(F32),
                                      ALU.subtract).then_inc(s_hl, 1)

                def pair_(i, it=0):
                    split(u0 + 1 + 2 * i + LEAD, it, 4)
                    for m in range(2):
                        relu2(g0 + 2 * i + 2 + m, up[:, (i + 1) % 2, m, :], it)
                    split(u0 + 2 + 2 * i + LEAD, it, 4)
                    hid_lo(i + 1, it)

                split(u0 + LEAD)
                for m in range(2):
                    relu2(g0 + m, up[:, 0, m, :])
                hid_lo(0)
                with dve.Fori(0, 7) as it:
                    pair_(0, it)
                    pair_(1, it)
                pair_(14)
                add_out((A_MLP0, A_MLP1)[layer], u0 + MLP_UNITS - 1)

            norm(2, res, [(XA, R_MLP)], late=U_ROUT + 3 + LEAD)
            mlp(0)

            norm(3, res, [(XA, R_KV), (XB, R_B)], late=U_MLP0 + MLP_UNITS - 1 + LEAD)
            for i in range(4):
                split(U_K + i + LEAD)

            def kq_out(r, u_last, bank):
                dve.wait_ge(s_step, AFTER[u_last])
                if r:
                    dve.wait_ge(s_kqT, 1)
                for t in range(TT):
                    ins = dve.tensor_copy(kq[:, t, :], PS[:, bank + 2 * t:bank + 2 * t + 2, :].rearrange("p a b -> p (a b)"))
                ins.then_inc(s_bev, 1)

            def kq_norm(r):
                dve.wait_ge(s_kq2, r + 1)
                link(dve.tensor_reduce(ss[:, 0:32], xn.rearrange("p t (h d) -> p (t h) d", d=64), AX_X, ALU.add))
                dve.tensor_scalar(ss[:, 32:64], ss[:, 0:32], EPS, None, ALU.add).then_inc(s_ms, 1)
                dve.wait_ge(s_rms, r + 1)
                link(dve.reciprocal(rstd[:, 0:32], rstd[:, 0:32]))
                v = kq.rearrange("p t (h d) -> p (t h) d", d=64)
                dve.tensor_tensor(v, v, rstd[:, 0:32].unsqueeze(2).to_broadcast([P, 32, 64]), ALU.mult)\
                   .then_inc(s_kqn, 1)

            split(U_Q + LEAD)
            kq_out(0, U_K + 3, 4)
            kq_norm(0)
            for i in range(1, 4):
                split(U_Q + i + LEAD)
            split(U_V + LEAD)
            kq_out(1, U_Q + 3, 0)
            kq_norm(1)
            for i in range(1, 3):
                split(U_V + i + LEAD)
            def row_max(H):
                pr, _, r = place_of(H)
                bank = score_bank(H)
                dve.wait_ge(s_S, H + 1)
                if H < 32:
                    if H >= 3:
                        dve.wait_ge(s_pt, H - 2)
                    h = H if H < 16 else H - 16
                    own, both = bias1[:, h, P - 1::-1], bias1[:, h, ::-1]
                    dve.tensor_tensor_reduce(pr[:, 0:P], PS[:, bank, 0:P], own, 1.0, -3.0e38, ALU.add,
                                             ALU.max, smax[:, r, 0:1])
                    ins = dve.tensor_tensor_reduce(pr[:, P:3 * P], PS[:, bank, P:3 * P], both, 1.0, -3.0e38,
                                                   ALU.add, ALU.max, smax[:, r, 1:2])
                    ins.then_inc(s_Sfree, 1)
                    dve.wait_ge(s_Sfree, H + 1)
                else:
                    link(dve.tensor_reduce(smax[:, r, :], PS[:, bank, :].rearrange("p (t n) -> p t n", t=TT), AX_X,
                                           ALU.max))
                if 24 <= H < 32:
                    link(dve.tensor_scalar(smax[:, r, :], smax[:, r, :], sinks[:, H - 24:H - 23], None, ALU.max))
                dve.tensor_scalar(snmax[:, r, :], smax[:, r, :], -1.0, None, ALU.mult).then_inc(s_max, 1)

            def norm_probs(H):
                pr, _, r = place_of(H)
                dve.wait_ge(s_exp, H + 1)
                if 24 <= H < 32:
                    link(dve.tensor_tensor(ssum[:, r, :], ssum[:, r, :], ssink[:, r, :], ALU.add))
                link(dve.reciprocal(srec[:, r, :], ssum[:, r, :]))
                w = P if H < 32 else T
                dve.tensor_scalar(pr[:, 0:w], pr[:, 0:w], srec[:, r, 0:1], None, ALU.mult)
                dve.tensor_scalar(pr[:, w:w + T], pr[:, w:w + T], srec[:, r, 1:2], None, ALU.mult).then_inc(s_p, 1)

            def attn_lo(H):
                if not ends_out(H):
                    return
                o = out_of(H)
                dve.wait_ge(s_ohi, o + 1)
                X, k = attn_dst(o)
                dve.tensor_tensor(X[:, k, 1, :], PS[:, out_bank(H), 0:T], X[:, k, 0, :].bitcast(F32), ALU.subtract)\
                   .then_inc(s_olo, 1)

            dve.wait_ge(s_b1, 1)
            row_max(0)
            row_max(1)
            for H in range(16):
                norm_probs(H)
                if H == 0:
                    dve.wait_ge(s_step, AFTER[U_V + 3])
                    dve.tensor_copy(vtok[:, 1, :], PS[:, 6:8, :].rearrange("p a b -> p (a b)")).then_inc(s_bev, 1)
                if H + 2 < 16:
                    row_max(H + 2)
                if H:
                    attn_lo(H - 1)
            attn_lo(15)
            add_out(A_O, U_O + 3)
            norm(4, res, [(XA, R_MLP + 8)], late=U_O + 3 + LEAD)
            mlp(1)

            norm(5, res, [(XA, R_MIX)], late=U_MLP1 + MLP_UNITS - 1 + LEAD)
            for i in range(6):
                split(U_QKV + i + LEAD)
            dve.wait_ge(s_step, AFTER[U_QKV + 5])
            dve.tensor_copy(v_mb, PS[:, 6:8, :]).then_inc(s_bev, 1)
            for i in range(6, 9):
                split(U_QKV + i + LEAD)
            dve.wait_ge(s_step, AFTER[U_QKV + 8])
            dve.tensor_copy(v_sw, PS[:, 5, 0:T].rearrange("p (t n) -> p t n", t=TT)).then_inc(s_bev, 1)
            for i in range(9, 11):
                split(U_QKV + i + LEAD)
            dve.wait_ge(s_b2, 2)

            def gates(b, k, H, last):
                if H <= last:
                    norm_probs(H)
                if H < last:
                    row_max(H + 1)
                if k % 2 == 0:
                    split(U_G2[b] + k // 2 + LEAD)
                if H - 1 <= last and k:
                    attn_lo(H - 1)

            def branch(b, k):
                g = G_BR[b] + k
                dve.wait_ge(s_step, BEFORE(U_BR[b]) + k + 1)
                dve.wait_ge(s_evac, g)
                if 8 * b + k >= 12:
                    dve.wait_ge(s_sum, 8 * b + k - 11)
                dst = merged[:, k, :] if b == 0 else ubr[:, g % 4, :]
                dve.scalar_tensor_tensor(dst, g_br[b][:, k, :], 1.0, PS[:, bank_of(g), 0:T], ALU.add, ALU.mult)\
                   .then_inc(s_evac, 1)

            row_max(16)
            for k in range(8):
                gates(0, k, 16 + k, 31)
            attn_lo(23)
            for k in range(8):
                gates(1, k, 24 + k, 31)
            branch(0, 0)
            attn_lo(31)
            for k in range(1, 8):
                branch(0, k)
                if k % 4 == 1:
                    split(U_BR[0] + k // 4 + LEAD)
            row_max(32)
            for k in range(8):
                gates(2, k, 32 + k, 35)

            def merged_lo(k):
                dve.wait_ge(s_mh, k + 1)
                dve.scalar_tensor_tensor(XA[:, 4 * k:4 * k + 4, 1, :], merged[:, 4 * k:4 * k + 4, :], 0.5,
                                         XA[:, 4 * k:4 * k + 4, 0, :].bitcast(F32), ALU.mult, ALU.subtract)\
                   .then_inc(s_ml, 1)

            for b in (1, 2):
                for k in range(8):
                    branch(b, k)
                    if k % 4 == 1:
                        split(U_BR[b] + k // 4 + LEAD)
                    if (b, k) == (2, 6):
                        merged_lo(0)
            merged_lo(1)
            for i in range(3):
                split(U_OUT2 + i + LEAD)

            def post(n):
                dve.wait_ge(s_gp, 32)
                for t in range(TT):
                    dve.wait_ge(s_rstd, ROOTS[SQ_POST[n]] + t + 1)
                    for c in range(2):
                        y, v = (x[:, t, 512 * c:512 * c + 512] for x in (xn, res))
                        link(dve.scalar_tensor_tensor(y, PS[:, 4 + 2 * t + c, :], rstd[:, t:t + 1],
                                                      gpost[:, n, 512 * c:512 * c + 512], ALU.mult, ALU.mult))
                        dve.tensor_tensor(v, v, y, ALU.add).then_inc(s_add, 1)

            post(0)
            norm(6, res, [(XA, R_FFN)], late=U_OUT2 + 3 + LEAD)
            for k in range(4):
                ins = dve.memset(fu[:, k, 0:2], 0.0)
            link(ins)

            def conv2(g0, e, j):
                dve.wait_ge(s_evac, g0 + 2)
                for i in range(2):
                    for m in range(2):
                        f, c = 2 * e + m, 44 * i + e * 22 + 2 * j + m
                        ins = dve.scalar_tensor_tensor(fc[:, f, :], fu[:, f, i:i + T], fvec[:, 0, c:c + 1],
                                                       fc[:, f, :], ALU.mult, ALU.add)
                    if i == 0:
                        link(ins)
                return ins

            for j in range(FFN_STEPS):
                u = U_FFN if j == 0 else U_FFN + 2 + 3 * (j - 1)
                for e in range(2):
                    split(u + e + LEAD)
                    conv2(G_FFN + 4 * j + 2 * e, e, j).then_inc(s_conv2, 1)
                dve.wait_ge(s_conv2, 2 * j + 2)
                dve.wait_ge(s_gelu2, j + 1)
                dve.tensor_tensor(fc[:, 0:2, :], fc[:, 0:2, :], fc[:, 2:4, :], ALU.mult).then_inc(s_prod, 1)
                k = 2 * (j % 2)
                dve.wait_ge(s_fh, j + 1)
                dve.tensor_tensor(XB[:, k:k + 2, 1, :], fc[:, 0:2, :], XB[:, k:k + 2, 0, :].bitcast(F32),
                                  ALU.subtract).then_inc(s_fl, 1)
                if j:
                    split(u + 2 + LEAD)
            post(1)



def bucket_onehot():
    n = np.maximum(np.arange(384) - P, 0)
    nf = np.maximum(n, 1).astype(np.float32)
    large = 16 + (np.log(nf / np.float32(16)) / np.float32(np.log(128 / 16)) * np.float32(16)).astype(np.int32)
    bucket = np.where(n < 16, n, np.minimum(large, 31))
    return (bucket[None, :] == np.arange(32)[:, None]).astype(np.float32)


_INS = ['x', 'a_norm', 'a_w_in', 'a_conv_w', 'a_conv_b', 'a_w_gate', 'a_b_gate', 'a_lambda', 'a_w_out', 'kv_norm',
        'w_kv', 'k_norm', 'b_norm', 'b_w_q', 'b_q_norm', 'b_rel_bias', 'b_w_o', 'mlp_norm', 'w_up', 'w_down', 'mem_2',
        'norm_mix_pre_2', 'norm_mix_post_2', 'norm_ffn_pre_2', 'norm_ffn_post_2', 'norm_mem_2', 'w_in_2', 'rel_bias_2',
        'swa_sinks_2', 'w_mem_kv_2', 'w_branch_moba_2', 'w_branch_swa_2', 'w_branch_mem_2', 'w_out_2', 'w_ffn_up_2',
        'ffn_conv_w_2', 'ffn_conv_b_2', 'w_ffn_down_2']


def kernel(**inputs):
    import numpy as _np
    import concourse.bacc as _bacc
    from concourse import mybir as _mybir
    from concourse.bass_utils import run_bass_kernel_spmd as _run

    nc = _bacc.Bacc("TRN2", target_bir_lowering=False, num_devices=1)
    arrays, A = {}, {}
    for name in _INS + ['bucket_onehot']:
        a = bucket_onehot() if name == 'bucket_onehot' else _np.asarray(inputs[name])
        a = _np.ascontiguousarray(a)
        arrays[f"in_{name}"] = a
        A[name] = nc.dram_tensor(f"in_{name}", a.shape, _mybir.dt.from_np(a.dtype), kind="ExternalInput").ap()
    out = nc.dram_tensor("out_0", (1, 256, 1024), _mybir.dt.float32, kind="ExternalOutput").ap()
    bass_blocks(nc, A, out)
    r = _run(nc, [arrays], core_ids=[0])
    return r.results[0]["out_0"]
```
